# Optimizing a Trainium2 kernel written in Bass

```python
import math
import jax, jax.numpy as jnp
from jax import lax
import numpy as np

D_MODEL = 1024
BATCH = 1
SEQ = 1024
DEPTH = 2
DEC_BATCH = 8
DEC_SEQ = 4
PAST_LEN = 8192
PAGE_SIZE = 128

N_EVEN = (DEPTH + 1) // 2
N_ODD = DEPTH // 2
H_A = 4
DK_A = 128
DV_A = 128
CONV_W = 4
CHUNK_A = 64
G_B = 4
DG_B = 128
CHUNK_B = 128
H_C = 4
DK_C = 128
DV_C = 256
CHUNK_C = 64
D_FF = 4 * D_MODEL
EPS = 1e-6

QK_A = H_A * DK_A
V_A = H_A * DV_A
CONV_CH = 2 * QK_A + V_A
W_B = G_B * DG_B
D_IN_EVEN = CONV_CH + V_A + 2 * H_A + 2 * W_B
D_MIX_EVEN = V_A + W_B
QK_C = H_C * DK_C
V_C = H_C * DV_C
D_IN_ODD = 2 * QK_C + V_C + 2 * H_C + V_C

kernel_name = 'hybrid_gdn_sgu_mlstm_step'

def rmsnorm(x, g):
    xf = x.astype(jnp.float32)
    y = xf * lax.rsqrt(jnp.mean(xf * xf, -1, keepdims=True) + EPS)
    return (y * g.astype(jnp.float32)).astype(x.dtype)

def l2norm(x):
    xf = x.astype(jnp.float32)
    return xf * lax.rsqrt(jnp.sum(xf * xf, -1, keepdims=True) + EPS)

def split_cols(x, sizes):
    outs, start = [], 0
    for s in sizes:
        outs.append(x[..., start:start + s])
        start += s
    return outs

def causal_mask(c, strict=False):
    r = jnp.arange(c)
    return (r[:, None] > r[None, :]) if strict else (r[:, None] >= r[None, :])

def to_blocks(t, nc, c):
    b, _, h = t.shape[:3]
    t = t.astype(jnp.float32).reshape((b, nc, c, h) + t.shape[3:])
    return jnp.moveaxis(t, (1, 3), (0, 2))

def from_blocks(o):
    nc, b, h, c, d = o.shape
    return jnp.moveaxis(o, (0, 2), (1, 3)).reshape(b, nc * c, h, d)

def short_conv(x, buf, w):
    L = x.shape[1]
    xp = jnp.concatenate([buf.astype(x.dtype), x], axis=1)
    y = sum(w[j] * xp[:, j:j + L] for j in range(CONV_W))
    return jax.nn.silu(y), xp[:, L:]

def gated_delta_rule(q, k, v, g, beta, S0):
    B, L, H, DK = q.shape
    DV = v.shape[-1]
    C = math.gcd(L, CHUNK_A)
    NC = L // C
    q = to_blocks(q, NC, C) * (DK ** -0.5)
    k = to_blocks(k, NC, C)
    v = to_blocks(v, NC, C)
    beta = to_blocks(beta, NC, C)
    gc = jnp.cumsum(to_blocks(g, NC, C), -1)
    causal = causal_mask(C)
    strict = causal_mask(C, strict=True)
    gdiff = jnp.where(causal, gc[..., :, None] - gc[..., None, :], 0.0)
    decay = jnp.where(causal, jnp.exp(gdiff), 0.0)
    kb = k * beta[..., None]
    A = jnp.where(strict, jnp.einsum('nbhid,nbhjd->nbhij', kb, k) * decay, 0.0)
    rhs = jnp.concatenate([v * beta[..., None], kb * jnp.exp(gc)[..., None]], -1)
    sol = lax.linalg.triangular_solve(jnp.eye(C, dtype=jnp.float32) + A, rhs,
                                      left_side=True, lower=True, unit_diagonal=True)
    u_val, w_k = sol[..., :DV], sol[..., DV:]
    qk = jnp.where(causal, jnp.einsum('nbhid,nbhjd->nbhij', q, k) * decay, 0.0)
    q_dec = q * jnp.exp(gc)[..., None]
    k_dec = k * jnp.exp(gc[..., -1:] - gc)[..., None]
    g_last = jnp.exp(gc[..., -1])

    def step(S, xs):
        u_c, wk_c, qk_c, qd_c, kd_c, gl_c = xs
        v_new = u_c - jnp.einsum('bhik,bhkv->bhiv', wk_c, S)
        o = jnp.einsum('bhik,bhkv->bhiv', qd_c, S) + jnp.einsum('bhij,bhjv->bhiv', qk_c, v_new)
        S = S * gl_c[..., None, None] + jnp.einsum('bhik,bhiv->bhkv', kd_c, v_new)
        return S, o

    S, o = lax.scan(step, S0.astype(jnp.float32), (u_val, w_k, qk, q_dec, k_dec, g_last))
    return from_blocks(o), S

def spatial_gating(u, v, w_s, b_s):
    B, L = u.shape[:2]
    C = min(L, CHUNK_B)
    NC = L // C
    w = jnp.where(causal_mask(C), w_s[:, :C, :C], 0.0)
    vc = v.reshape(B, NC, C, G_B, DG_B)
    z = jnp.einsum('gpq,bnqgc->bnpgc', w, vc) + b_s[:, :C].T[None, None, :, :, None]
    return u * z.reshape(u.shape).astype(u.dtype)

def mlstm_chunked(q, k, v, i_pre, f_pre, C0, n0, m0):
    B, L, H, DK = q.shape
    Cs = math.gcd(L, CHUNK_C)
    NC = L // Cs
    q = to_blocks(q, NC, Cs) * (DK ** -0.5)
    k = to_blocks(k, NC, Cs)
    v = to_blocks(v, NC, Cs)
    ig = to_blocks(i_pre, NC, Cs)
    bcum = jnp.cumsum(jax.nn.log_sigmoid(to_blocks(f_pre, NC, Cs)), -1)
    causal = causal_mask(Cs)

    def step(carry, xs):
        Cm, n, m = carry
        q_c, k_c, v_c, i_c, b_c = xs
        inter = b_c + m[..., None]
        dmat = jnp.where(causal, b_c[..., :, None] - b_c[..., None, :] + i_c[..., None, :], -jnp.inf)
        m_t = jnp.maximum(inter, jnp.max(dmat, -1))
        w_intra = jnp.exp(dmat - m_t[..., None])
        w_inter = jnp.exp(inter - m_t)
        s = jnp.einsum('bhid,bhjd->bhij', q_c, k_c) * w_intra
        num = w_inter[..., None] * jnp.einsum('bhid,bhdv->bhiv', q_c, Cm) + jnp.einsum('bhij,bhjv->bhiv', s, v_c)
        den = w_inter * jnp.einsum('bhid,bhd->bhi', q_c, n) + jnp.sum(s, -1)
        h = num / jnp.maximum(jnp.abs(den), jnp.exp(-m_t))[..., None]
        b_last = b_c[..., -1]
        log_w = b_last[..., None] - b_c + i_c
        m_new = jnp.maximum(b_last + m, jnp.max(log_w, -1))
        keep = jnp.exp(b_last + m - m_new)
        wk = jnp.exp(log_w - m_new[..., None])
        Cm = keep[..., None, None] * Cm + jnp.einsum('bhj,bhjd,bhjv->bhdv', wk, k_c, v_c)
        n = keep[..., None] * n + jnp.einsum('bhj,bhjd->bhd', wk, k_c)
        return (Cm, n, m_new), h

    init = (C0.astype(jnp.float32), n0.astype(jnp.float32), m0.astype(jnp.float32))
    (Cm, n, m), h = lax.scan(step, init, (q, k, v, ig, bcum))
    return from_blocks(h), Cm, n, m

def even_mixer(h, S0, conv_buf, w_in, conv_w, a_log, dt_bias, gdn_norm_g, sgu_norm_g, sgu_w, sgu_b, w_out):
    B, L, _ = h.shape
    proj = h @ w_in
    qkv, gate, beta_pre, a_pre, u_pre, v_pre = split_cols(proj, (CONV_CH, V_A, H_A, H_A, W_B, W_B))
    qkv_c, new_buf = short_conv(qkv, conv_buf, conv_w)
    q, k, v = split_cols(qkv_c, (QK_A, QK_A, V_A))
    q = l2norm(q.reshape(B, L, H_A, DK_A))
    k = l2norm(k.reshape(B, L, H_A, DK_A))
    v = v.reshape(B, L, H_A, DV_A)
    beta = jax.nn.sigmoid(beta_pre.astype(jnp.float32))
    g = -jnp.exp(a_log.astype(jnp.float32)) * jax.nn.softplus(a_pre.astype(jnp.float32) + dt_bias.astype(jnp.float32))
    o, S = gated_delta_rule(q, k, v, g, beta, S0)
    o_a = rmsnorm(o, gdn_norm_g) * jax.nn.silu(gate.reshape(B, L, H_A, DV_A).astype(jnp.float32))
    o_a = o_a.reshape(B, L, V_A).astype(h.dtype)
    u = jax.nn.gelu(u_pre, approximate=False).reshape(B, L, G_B, DG_B)
    vb = rmsnorm(jax.nn.gelu(v_pre, approximate=False).reshape(B, L, G_B, DG_B), sgu_norm_g)
    o_b = spatial_gating(u, vb, sgu_w, sgu_b).reshape(B, L, W_B)
    out = jnp.concatenate([o_a, o_b], -1) @ w_out
    return out, S, new_buf, vb.reshape(B, L, W_B)

def odd_mixer(h, C0, n0, m0, w_in, gate_b, head_norm_g, w_out):
    B, L, _ = h.shape
    proj = h @ w_in
    q, k, v, i_pre, f_pre, o_pre = split_cols(proj, (QK_C, QK_C, V_C, H_C, H_C, V_C))
    i_pre = i_pre.astype(jnp.float32) + gate_b[:H_C]
    f_pre = f_pre.astype(jnp.float32) + gate_b[H_C:]
    hh, Cm, n, m = mlstm_chunked(q.reshape(B, L, H_C, DK_C), k.reshape(B, L, H_C, DK_C),
                                 v.reshape(B, L, H_C, DV_C), i_pre, f_pre, C0, n0, m0)
    hh = rmsnorm(hh, head_norm_g) * jax.nn.sigmoid(o_pre.reshape(B, L, H_C, DV_C).astype(jnp.float32))
    out = hh.reshape(B, L, V_C).astype(h.dtype) @ w_out
    return out, Cm, n, m

def squared_relu_mlp(h, w1, w2):
    return jnp.square(jax.nn.relu(h @ w1)) @ w2

def trunk(x, s_gdn, s_conv, s_c, s_n, s_m, norm_g, w_in_even, conv_w, a_log, dt_bias, gdn_norm_g,
          sgu_norm_g, sgu_w, sgu_b, w_out_even, w_in_odd, gate_b_odd, mlstm_norm_g, w_out_odd, w_ff1, w_ff2):
    new_gdn, new_conv, new_v, new_c, new_n, new_m = [], [], [], [], [], []
    for l in range(DEPTH):
        gl = norm_g[l]
        h = rmsnorm(x, gl[0])
        if l % 2 == 0:
            e = l // 2
            mix, S, buf, vrows = even_mixer(h, s_gdn[e], s_conv[e], w_in_even[e], conv_w[e], a_log[e], dt_bias[e],
                                            gdn_norm_g[e], sgu_norm_g[e], sgu_w[e], sgu_b[e], w_out_even[e])
            new_gdn.append(S)
            new_conv.append(buf)
            new_v.append(vrows)
        else:
            o = l // 2
            mix, Cm, n, m = odd_mixer(h, s_c[o], s_n[o], s_m[o], w_in_odd[o], gate_b_odd[o], mlstm_norm_g[o], w_out_odd[o])
            new_c.append(Cm)
            new_n.append(n)
            new_m.append(m)
        x = x + rmsnorm(mix, gl[1])
        h = rmsnorm(x, gl[2])
        x = x + rmsnorm(squared_relu_mlp(h, w_ff1[l], w_ff2[l]), gl[3])
    return (x, jnp.stack(new_gdn), jnp.stack(new_conv), jnp.stack(new_v),
            jnp.stack(new_c), jnp.stack(new_n), jnp.stack(new_m))

def setup_inputs(seed: int = 0) -> dict:
    key = jax.random.key(seed)
    ks = jax.random.split(key, 24)
    nrm = jax.random.normal
    f32 = jnp.float32
    x_prompt = nrm(ks[0], (BATCH, SEQ, D_MODEL), f32)
    x_sample = nrm(ks[1], (DEC_BATCH, DEC_SEQ, D_MODEL), f32)
    state_gdn = 0.05 * nrm(ks[2], (N_EVEN, DEC_BATCH, H_A, DK_A, DV_A), f32)
    state_gdn_conv = nrm(ks[3], (N_EVEN, DEC_BATCH, CONV_W - 1, CONV_CH), f32)
    state_mlstm_c = 0.1 * nrm(ks[4], (N_ODD, DEC_BATCH, H_C, DK_C, DV_C), f32)
    state_mlstm_n = 0.1 * nrm(ks[5], (N_ODD, DEC_BATCH, H_C, DK_C), f32)
    state_mlstm_m = nrm(ks[6], (N_ODD, DEC_BATCH, H_C), f32)
    norm_g = 1.0 + 0.05 * nrm(ks[7], (DEPTH, 4, D_MODEL), f32)
    w_in_even = nrm(ks[8], (N_EVEN, D_MODEL, D_IN_EVEN), f32) * D_MODEL ** -0.5
    conv_w = 0.5 * nrm(ks[9], (N_EVEN, CONV_W, CONV_CH), f32)
    a_log = jnp.log(jax.random.uniform(ks[10], (N_EVEN, H_A), f32, 1.0, 16.0))
    dt = jnp.exp(jax.random.uniform(ks[11], (N_EVEN, H_A), f32, math.log(1e-3), math.log(1e-1)))
    dt_bias = dt + jnp.log(-jnp.expm1(-dt))
    gdn_norm_g = 1.0 + 0.05 * nrm(ks[12], (N_EVEN, DV_A), f32)
    sgu_norm_g = 1.0 + 0.05 * nrm(ks[13], (N_EVEN, G_B, DG_B), f32)
    sgu_w = nrm(ks[14], (N_EVEN, G_B, CHUNK_B, CHUNK_B), f32) * CHUNK_B ** -0.5
    sgu_b = 1.0 + 0.1 * nrm(ks[15], (N_EVEN, G_B, CHUNK_B), f32)
    w_out_even = nrm(ks[16], (N_EVEN, D_MIX_EVEN, D_MODEL), f32) * D_MIX_EVEN ** -0.5
    w_in_odd = nrm(ks[17], (N_ODD, D_MODEL, D_IN_ODD), f32) * D_MODEL ** -0.5
    gate_b_odd = jnp.concatenate([0.1 * nrm(ks[18], (N_ODD, H_C), f32),
                                  3.0 + 0.5 * nrm(ks[19], (N_ODD, H_C), f32)], -1)
    mlstm_norm_g = 1.0 + 0.05 * nrm(ks[20], (N_ODD, DV_C), f32)
    w_out_odd = nrm(ks[21], (N_ODD, V_C, D_MODEL), f32) * V_C ** -0.5
    w_ff1 = nrm(ks[22], (DEPTH, D_MODEL, D_FF), f32) * D_MODEL ** -0.5
    w_ff2 = nrm(ks[23], (DEPTH, D_FF, D_MODEL), f32) * D_FF ** -0.5
    return {'x_prompt': x_prompt, 'x_sample': x_sample,
            'state_gdn': state_gdn, 'state_gdn_conv': state_gdn_conv,
            'state_mlstm_c': state_mlstm_c, 'state_mlstm_n': state_mlstm_n, 'state_mlstm_m': state_mlstm_m,
            'norm_g': norm_g, 'w_in_even': w_in_even, 'conv_w': conv_w, 'a_log': a_log, 'dt_bias': dt_bias,
            'gdn_norm_g': gdn_norm_g, 'sgu_norm_g': sgu_norm_g, 'sgu_w': sgu_w, 'sgu_b': sgu_b,
            'w_out_even': w_out_even, 'w_in_odd': w_in_odd, 'gate_b_odd': gate_b_odd,
            'mlstm_norm_g': mlstm_norm_g, 'w_out_odd': w_out_odd, 'w_ff1': w_ff1, 'w_ff2': w_ff2}

def reference(x_prompt, x_sample, state_gdn, state_gdn_conv, state_mlstm_c, state_mlstm_n, state_mlstm_m,
              norm_g, w_in_even, conv_w, a_log, dt_bias, gdn_norm_g, sgu_norm_g, sgu_w, sgu_b, w_out_even,
              w_in_odd, gate_b_odd, mlstm_norm_g, w_out_odd, w_ff1, w_ff2):
    f32 = jnp.float32
    bp = x_prompt.shape[0]
    y_prompt, p_gdn, p_conv, _, p_c, p_n, p_m = trunk(
        x_prompt,
        jnp.zeros((N_EVEN, bp, H_A, DK_A, DV_A), f32),
        jnp.zeros((N_EVEN, bp, CONV_W - 1, CONV_CH), x_prompt.dtype),
        jnp.zeros((N_ODD, bp, H_C, DK_C, DV_C), f32),
        jnp.zeros((N_ODD, bp, H_C, DK_C), f32),
        jnp.zeros((N_ODD, bp, H_C), f32),
        norm_g, w_in_even, conv_w, a_log, dt_bias, gdn_norm_g, sgu_norm_g, sgu_w, sgu_b, w_out_even,
        w_in_odd, gate_b_odd, mlstm_norm_g, w_out_odd, w_ff1, w_ff2)
    y_sample, s_gdn, s_conv, s_v, s_c, s_n, s_m = trunk(
        x_sample, state_gdn, state_gdn_conv, state_mlstm_c, state_mlstm_n, state_mlstm_m,
        norm_g, w_in_even, conv_w, a_log, dt_bias, gdn_norm_g, sgu_norm_g, sgu_w, sgu_b, w_out_even,
        w_in_odd, gate_b_odd, mlstm_norm_g, w_out_odd, w_ff1, w_ff2)
    return (y_prompt, y_sample, p_gdn, s_gdn, p_conv, s_conv, s_v, p_c, s_c, p_n, s_n, p_m, s_m)


_drawn_inputs = setup_inputs


def setup_inputs(seed=0):
    import zlib

    import numpy as np

    out = dict(_drawn_inputs(seed))
    spreads = {}
    factors = {}
    for name, (base, spread) in spreads.items():
        noise = np.random.default_rng([zlib.crc32(name.encode()), seed]).standard_normal(out[name].shape)
        drawn = base * np.exp(spread * noise) if base else spread * noise
        out[name] = __import__('jax').numpy.asarray(drawn.astype(out[name].dtype))
    for name, factor in factors.items():
        out[name] = (out[name] * factor).astype(out[name].dtype)
    return out
```

```python
from contextlib import ExitStack

import concourse.bass as bass
from concourse import mybir

F32 = mybir.dt.float32
F32R = mybir.dt.float32r
ALU = mybir.AluOpType
ACT = mybir.ActivationFunctionType

P = 128
D = 1024
KT = D // P
NP = 1024
NB, LS = 8, 4
NS = NB * LS
T = NP + NS
TG = 3
N = T // TG
TILES = NP // P
H = 4
DFF = 4 * D
CONVW = 4
NCONV = 12
NCH = 24
GATE0 = 2048
DV = 256
EPS = 1e-6
BIG = 1e30
QSCALE = P ** -0.5
LEVELS = 7
LEVELS_S = 2
XC = 3 + NP
XCW = XC + NB * (3 + LS)
FG = 8
FK = DFF // P // FG

U_IN, U_OUT, U_FF = NCH, KT, FG * 2 * FK
U_LAYER = U_IN + U_OUT + U_FF
J_IN, J_OUT, J_W1, J_W2 = TG * NCH, TG * KT, TG * FK, TG * KT
J_LAYER = J_IN + J_OUT + FG * (J_W1 + J_W2)
A_LAYER = J_IN + J_OUT + FG * J_W1
D_LAYER = FG * J_W2
BANKS = 6


def build(nc, x_prompt, x_sample, state_gdn, state_gdn_conv, state_mlstm_c, state_mlstm_n, state_mlstm_m,
          norm_g, w_in_even, conv_w, a_log, dt_bias, gdn_norm_g, sgu_norm_g, sgu_w, sgu_b, w_out_even,
          w_in_odd, gate_b_odd, mlstm_norm_g, w_out_odd, w_ff1, w_ff2,
          y_prompt, y_sample, gdn_p, gdn_s, conv_p, conv_s, sguv_s, c_p, c_s, n_p, n_s, m_p, m_s):
    ctx = ExitStack()
    with ctx:
        sems = {}

        def S(name):
            if name not in sems:
                sems[name] = ctx.enter_context(nc.semaphore(name))
            return sems[name]

        def sb(name, shape, dt=F32):
            return ctx.enter_context(nc.sbuf_tensor(name, shape, dt))

        xT = sb("xT", [P, KT, T])
        hhi = sb("hhi", [P, KT, T], F32R)
        hlo = sb("hlo", [P, KT, T], F32R)
        wst = sb("wst", [P, 2, 1024])
        whi = sb("whi", [P, 2, 1024], F32R)
        wlo = sb("wlo", [P, 2, 1024], F32R)
        arena_at = -(-nc.sbuf_base // 32) * 32
        arena = sb("arena", [P, 2 * KT * T])

        ident = sb("ident", [P, P])
        ones = sb("ones", [P, P])
        maskpos = sb("maskpos", [P, P])
        masknegT = sb("masknegT", [P, P])
        maskposS = sb("maskposS", [NS, NS])
        masknegTS = sb("masknegTS", [NS, NS])
        triU = sb("triU", [P, P])
        triUS = sb("triUS", [NS, NS])
        blk4 = sb("blk4", [NS, NS])
        lmask = sb("lmask", [P, LEVELS, P])
        rowmask = sb("rowmask", [NS, NB])
        colmask = sb("colmask", [P, NB, NS])
        sel = sb("sel", [H, H, P])
        par = sb("par", [P, P])
        gates = sb("gates", [P, TILES + 1, 2 * H])
        wg = sb("wg", [P, KT, 2 * H])
        cols = sb("cols", [P, TILES + 1, 6, H])
        tcol = sb("tcol", [P, 6, H])
        small = sb("small", [P, 8, H])
        gtmp = sb("gtmp", [P, 4, (TILES + 1) * H])
        hvec = sb("hvec", [P, 4, H])
        keepb = sb("keepb", [P, H, 2 * NB])
        epsc = sb("epsc", [P, 1])
        rows4 = sb("rows4", [H, 2, P])

        def psum(name):
            return ctx.enter_context(nc.psum_tensor(name, [P, 512], F32))

        B = [psum(f"bank{i}") for i in range(8)]

        def B4(i):
            return B[i][:, :].rearrange("p (h n) -> p h n", h=4)


        def carve(*shapes, at=0):
            out = []
            for shape in shapes:
                size = 1
                for s in shape:
                    size *= s
                v = arena[:, at:at + size]
                if len(shape) > 1:
                    names = "abcd"[:len(shape)]
                    v = v.rearrange("p (" + " ".join(names) + ") -> p " + " ".join(names),
                                    **dict(zip(names, shape)))
                out.append(v)
                at += size
            assert at <= 2 * KT * T, at
            return out

        acc, sq2, ssum, lnss, rstd, hf2 = carve((KT, T), (2, T), (T,), (T,), (T,), (2, T))
        half = arena_at + 4 * KT * T
        h1hi = nc.alloc_sbuf_tensor_at("h1hi", [P, FK, T], F32R, offset=half)
        h1lo = nc.alloc_sbuf_tensor_at("h1lo", [P, FK, T], F32R, offset=half + 4 * FK * T)
        x_tm, rows_in = carve((2, D), (P,))
        xc2, cy2, pout2, cs_tm = carve((2, XCW), (2, T), (2, T), (NCONV * P,))
        tail_tm = carve((NCONV * P,), at=KT * T)[0]
        csT, tails, cw2 = carve((NCONV, NB * 3), (NCONV, 3 + NB * 3), (2, CONVW), at=(KT + 7) * T)
        St, GR, WT, WTS, BROW, BROWS, GSG, gdn_end = carve(
            (H, P), (T,), (H, P), (H, NS), (H, P), (H, NB, LS), (H, P), (1,))
        gdn_at = 4 * 512 + T + 2 * H * NS
        sgw_in = carve((H, P), at=8192)[0]
        CN, ROWM, ROWW = carve((H, DV + 1), (T,), (T,))
        ml_at = H * (DV + 1) + 2 * T + 4
        IR, LF, BR, MR, AR, LWR, RST, MSX, D0X, D1X, MPR, MLA, BLA, KPR, fixr = carve(
            (T,), (T,), (T,), (T,), (T,), (T,), (T,), (NB, LS + 1), (NB, LS + 1), (NB, LS + 1),
            (2 * NB,), (2 * NB,), (2 * NB,), (2 * NB,), (4,), at=ml_at)
        relu2 = sb("relu2", [P, 2, N])
        cum = sb("cum", [P, TILES + 1, 12])

        def gdn_map(n):
            keys = ["X", "QH", "SQ", "RB", "OF", "DT", "A", "Xi", "XiT", "RW", "KD", "RU", "VN", "ON", "VB"]
            shapes = [(NCH, n), (8, n), (8, n), (8, n), (8, n)] + [(H, n)] * 4 + [(H, P)] * 6
            if n == NS:
                keys += ["SS", "NWM", "QDM", "VNM"]
                shapes += [(NB, H, P), (H, NB, NS), (H, NB, NS), (NB, P)]
            m = dict(zip(keys, carve(*shapes, at=gdn_at)))
            m["Dm"], m["E"] = m["SQ"][:, 0:4], m["SQ"][:, 4:8]
            m["T2"], m["NW"] = m["RB"][:, 0:4], m["RB"][:, 4:8]
            m["QD"] = m["E"]
            return m

        def ml_map(n):
            keys = ["X", "WTm", "E", "QD", "ST", "OF", "KW", "V1", "HN"]
            shapes = [(NCH, n), (H, n), (H, n), (H, n), (H, n), (8, n), (H, P), (H, DV + 1), (H, DV)]
            if n == NS:
                keys += ["CS2", "QDM", "VM"]
                shapes += [(2, NB, DV + 1), (H, NB, NS), (NB, DV + 1)]
            return dict(zip(keys, carve(*shapes, at=ml_at)))

        proj = [nc.dram_tensor(f"proj{l}", (NCH, P, T), F32) for l in range(2)]

        def accd(c, tg):
            return acc[:, bass.ds(c, 1), tg * N:(tg + 1) * N]

        phases = {}

        def phase_end(eng, who):
            phases[who] = phases.get(who, 0) + 1
            eng.drain().then_inc(S("phase_end"), 1)
            eng.wait_ge(S("phase_end"), 4 * phases[who])

        w_in = [w_in_even, w_in_odd]
        w_out = [w_out_even, w_out_odd]
        U0 = [0, U_LAYER]
        J0 = [0, J_LAYER]
        AE0 = [0, A_LAYER]
        DE0 = [0, D_LAYER]

        def in_cols(c):
            return c * P + (2 * H if c >= GATE0 // P else 0)

        block = ctx.enter_context(nc.Block())

        @block.sync
        def _(sp):
            def load(u, k, src):
                sp.wait_ge(S("w_split"), u + 1)
                dst = wst[:, k % 2, :]
                if len(src.shape) == 3:
                    dst = dst.rearrange("p (a b) -> p a b", a=src.shape[1])
                sp.dma_start(dst, src).then_inc(S(f"w_loaded{k % 2}"), 16)

            def cols_of(w, c0):
                return w[:, bass.ds(c0, P)].rearrange("(t p) n -> p t n", p=P)

            for l in range(2):
                u = U0[l]
                with sp.Fori(0, 8) as i:
                    for k in range(2):
                        load(i * 2 + (u + k), k, cols_of(w_in[l][0], i * (2 * P) + k * P))
                with sp.Fori(0, 4) as i:
                    for k in range(2):
                        load(i * 2 + (u + 16 + k), k, cols_of(w_in[l][0], i * (2 * P) + (in_cols(16) + k * P)))
                with sp.Fori(0, 4) as i:
                    for k in range(2):
                        load(i * 2 + (u + U_IN + k), k, cols_of(w_out[l][0], i * (2 * P) + k * P))
                with sp.Fori(0, FG) as g:
                    ug = u + U_IN + U_OUT
                    for k in range(FK):
                        load(g * (2 * FK) + (ug + k), k, cols_of(w_ff1[l], g * (FK * P) + k * P))
                    for k in range(FK):
                        rows = w_ff2[l][bass.ds(g * (FK * P), FK * P), 2 * k * P:2 * (k + 1) * P]
                        load(g * (2 * FK) + (ug + FK + k), k, rows.rearrange("(t p) n -> p t n", p=P))

        @block.tensor
        def _(pe):
            def mm(out, lhsT, rhs, start=True, stop=True):
                return pe.matmul(out, lhsT, rhs, start=start, stop=stop)

            def job(bank, kt, w, x, tg):
                n = 0
                for (a, b) in ((whi, x[0]), (whi, x[1]), (wlo, x[0])):
                    for t in range(kt):
                        last = mm(B[bank][:, 0:N], w(a, t), b[:, t, tg * N:(tg + 1) * N],
                                  start=n == 0, stop=n == 3 * kt - 1)
                        n += 1
                return last

            def w_ready(u):
                pe.wait_ge(S("w_split"), u + 3)

            def unit8(u, k, wait_bank):
                w_ready(u)
                for tg in range(TG):
                    b = (k % 2) * TG + tg
                    wait_bank(k * TG + tg)
                    last = job(b, KT, lambda a, t: a[:, k % 2, t * P:(t + 1) * P], (hhi, hlo), tg)
                    last.then_inc(S("job_done"), 1)
                pe.drain().then_inc(S("w_used"), 1)

            def linear(u0, a0, iters):
                with pe.Fori(0, iters) as i:
                    for k in range(2):
                        unit8(i * 2 + (u0 + k), k,
                              lambda j: pe.wait_ge(S("act_evac"), i * BANKS + (a0 + j + 1)))

            def to_cols(n, count, tile):
                pass

            def load_x():
                pe.wait_ge(S("ident_ready"), 1)
                pe.wait_ge(S("rows_loaded"), 16 * 6)
                pe.transpose(B[6][:, 0:P], rows_in[:, 0:P], ident[:, :]).then_inc(S("par_T"), 1)
                with pe.Fori(0, TILES // 2) as i:
                    for k in range(2):
                        pe.wait_ge(S(f"x_loaded{k}"), i * 16 + 16)
                        for q in range(2):
                            pe.wait_ge(S("xT_copied"), i * 4 + (2 * k + q + 1))
                            for c in range(4):
                                last = pe.transpose(B[2 * k + q][:, c * P:(c + 1) * P],
                                                    x_tm[:, k, (4 * q + c) * P:(4 * q + c + 1) * P], ident[:, :])
                            last.then_inc(S("x_turned"), 1)
                pe.wait_ge(S("x_loaded0"), 16 * (TILES // 2 + 1))
                for q in range(2):
                    pe.wait_ge(S("xT_copied"), 2 * TILES + q + 1)
                    for c in range(4):
                        last = pe.transpose(B[q][:, c * NS:(c + 1) * NS],
                                            x_tm[0:NS, 0, (4 * q + c) * P:(4 * q + c + 1) * P], ident[0:NS, 0:NS])
                    last.then_inc(S("x_turned"), 1)

            def norm(nn):
                pe.wait_ge(S("squares_added"), KT * (nn + 1))
                for tg in range(TG):
                    last = mm(B[tg][:, 0:N], ones[:, :], ssum[:, tg * N:(tg + 1) * N])
                last.then_inc(S("sumsq"), 1)

            def gate_cols(l):
                pe.wait_ge(S("h_split"), KT * (2 * l + 1 + l * 0) if l == 0 else KT * 3)
                pe.wait_ge(S("wg_loaded"), 16 * (2 + 2 * l))
                for t in range(TILES + 1):
                    n = P if t < TILES else NS
                    k = 0
                    for c in range(KT):
                        for part in (hhi, hlo):
                            last = mm(B[6][0:n, t * 8:t * 8 + 8], part[:, c, t * P:t * P + n].bitcast(F32),
                                      wg[:, c, :], start=k == 0, stop=k == 2 * KT - 1)
                            k += 1
                last.then_inc(S("gates_done"), 1)

            def ff(l):
                u0 = U0[l] + U_IN + U_OUT
                a0 = AE0[l] + J_IN + J_OUT
                d0 = DE0[l]
                pe.wait_ge(S("h_split"), KT * (2 * l + 2))
                pe.wait_ge(S("acc_zero"), l + 1)
                with pe.Fori(0, FG) as g:
                    def bank1(j):
                        if j < BANKS:
                            pe.wait_ge(S("dve_evac"), g * J_W2 + (d0 + j + 1))
                        else:
                            pe.wait_ge(S("act_evac"), g * J_W1 + (a0 + j + 1))
                    for k in range(FK):
                        unit8(g * (2 * FK) + (u0 + k), k, bank1)
                    pe.wait_ge(S("h1_split"), g * J_W1 + (l * FG * J_W1 + J_W1 + 2))
                    for k in range(FK):
                        w_ready(g * (2 * FK) + (u0 + FK + k))
                        for oc in range(2):
                            for tg in range(TG):
                                j = (2 * k + oc) * TG + tg
                                if j >= BANKS:
                                    pe.wait_ge(S("dve_evac"), g * J_W2 + (d0 + j + 1))
                                job(j % BANKS, FK,
                                    lambda a, t: a[:, k % 2, t * 2 * P + oc * P:t * 2 * P + (oc + 1) * P],
                                    (h1hi, h1lo), tg).then_inc(S("job_done"), 1)
                        pe.drain().then_inc(S("w_used"), 1)

            def conv_tails():
                pe.wait_ge(S("tails_ready"), 2 + NCONV)
                pe.wait_ge(S("act_evac"), BANKS + J_IN)
                for c in range(NCONV):
                    last = pe.transpose(B[c // 4][0:27, (c % 4) * P:(c % 4 + 1) * P], tails[:, c, :], ident[:, :])
                last.then_inc(S("tails_T"), 1)

            def gdn_prep():
                pe.wait_ge(S("cols_g"), 1)
                mm(B[7][:, 0:32], triU[:, :], cols[:, 0:TILES, 5, :])
                mm(B[7][0:NS, 32:36], triUS[:, :], cols[0:NS, TILES, 5, :])
                mm(B[7][:, 36:68], ones[:, :], cols[:, 0:TILES, 5, :])
                mm(B[7][0:NS, 68:72], blk4[:, :], cols[0:NS, TILES, 5, :])
                pe.wait_ge(S("gmask_ready"), 1)
                mm(B[7][:, 72:104], ones[0:NS, :], gtmp[0:NS, 3, 0:32]).then_inc(S("cum_done"), 1)
                pe.wait_ge(S("gc_ready"), 1)
                for t in range(TILES + 1):
                    n = P if t < TILES else NS
                    last = pe.transpose(B[t // 4][0:H, (t % 4) * P:(t % 4) * P + n], cols[0:n, t, 0, :],
                                        ident[0:n, 0:n])
                last.then_inc(S("gc_rows"), 1)
                pe.wait_ge(S("sgw_loaded"), 16 * (4 + NB))
                for g in range(H):
                    pe.transpose(B4(3)[:, g, :], sgw_in[:, g, :], ident[:, :])
                    last = pe.transpose(B[4][0:NS, g * NS:(g + 1) * NS], WTS[0:NS, g, :], ident[0:NS, 0:NS])
                last.then_inc(S("sgw_T"), 1)

            def gdn(t, n, lv, lv0):
                m = gdn_map(n)
                X, QH, SQ, OF = m["X"], m["QH"], m["SQ"], m["OF"]
                w = lambda name, v=None: pe.wait_ge(S("g_" + name), t + 1 if v is None else v)
                s = lambda ins, name: ins.then_inc(S("g_" + name), 1)
                w("sq")
                mm(B4(0)[:, :, 0:n], ones[:, :], SQ[:, 0:4, :])
                s(mm(B4(1)[:, :, 0:n], ones[:, :], SQ[:, 4:8, :]), "ss")
                for g in range(H):
                    last = pe.transpose(B4(7)[0:n, g, :], X[:, 20 + g, :], ident[:, :])
                s(last, "vsT")
                w("gr")
                for h in range(H):
                    last = mm(B4(2)[:, h, 0:n], sel[:, h, :], rows4[:, 0, 0:n])
                s(last, "bc")
                for h in range(H):
                    last = pe.transpose(B4(6)[0:n, h, :], X[:, 8 + h, :], ident[:, :])
                s(last, "vT")
                w("kn")
                for h in range(H):
                    last = mm(B4(3)[0:n, h, 0:n], QH[:, 4 + h, :], QH[:, 4 + h, :])
                s(last, "kk")
                w("qn")
                for h in range(H):
                    last = mm(B4(4)[0:n, h, 0:n], QH[:, 4 + h, :], QH[:, h, :])
                s(last, "kq")
                for h in range(H):
                    last = pe.transpose(B4(5)[0:n, h, :], QH[:, 4 + h, :], ident[:, :])
                s(last, "kT")
                w("vb")
                w("A")
                wt, br = (WT, BROW) if n == P else (WTS, BROWS.rearrange("p g b l -> p g (b l)"))
                for g in range(H):
                    mm(B4(3)[:, g, 0:n], m["VB"][0:n, g, :], wt[0:n, g, 0:n], start=True, stop=False)
                    last = mm(B4(3)[:, g, 0:n], ones[0:1, :], br[0:1, g, 0:n], start=False, stop=True)
                s(last, "z")
                w("Xinit")
                for q in range(lv):
                    if q:
                        w("inv", lv0 + q)
                    for h in range(H):
                        last = mm(B4(0)[0:n, h, 0:n], m["A"][0:n, h, :], m["XiT"][0:n, h, :])
                    s(last, "t2")
                    w("t2s", lv0 + q + 1)
                    for h in range(H):
                        last = mm(B4(1)[0:n, h, 0:n], m["T2"][0:n, h, :], m["Xi"][0:n, h, :])
                    s(last, "x1")
                    for h in range(H):
                        last = mm(B4(2)[0:n, h, 0:n], m["Xi"][0:n, h, :], m["T2"][0:n, h, :])
                    s(last, "x2")
                w("inv", lv0 + lv)
                w("rhs")
                w("ofb")
                for h in range(H):
                    last = mm(B4(3)[:, h, 0:n], m["RW"][0:n, h, :], m["XiT"][0:n, h, :])
                s(last, "w")
                w("state")
                w("nw")
                w("qk")
                for h in range(H):
                    mm(B4(4)[0:n, h, :], m["XiT"][0:n, h, :], m["RU"][0:n, h, :], start=True, stop=False)
                    if n == P:
                        last = mm(B4(4)[0:n, h, :], m["NW"][:, h, :], St[:, h, :], start=False, stop=True)
                    else:
                        for b in range(NB):
                            last = mm(B4(4)[0:n, h, :], m["NWM"][:, h, b, :], m["SS"][:, b, h, :],
                                      start=False, stop=b == NB - 1)
                s(last, "vnew")
                w("vns")
                w("qd")
                for h in range(H):
                    if n == P:
                        mm(B4(5)[0:n, h, :], m["QD"][:, h, :], St[:, h, :], start=True, stop=False)
                    else:
                        for b in range(NB):
                            mm(B4(5)[0:n, h, :], m["QDM"][:, h, b, :], m["SS"][:, b, h, :],
                               start=b == 0, stop=False)
                    last = mm(B4(5)[0:n, h, :], m["DT"][0:n, h, :], m["VN"][0:n, h, :], start=False, stop=True)
                s(last, "o")
                if n == P:
                    for h in range(H):
                        last = mm(B4(6)[:, h, :], m["KD"][:, h, :], m["VN"][:, h, :])
                    s(last, "ds")
                w("on")
                for h in range(H):
                    last = pe.transpose(B4(7)[:, h, 0:n], m["ON"][0:n, h, :], ident[0:n, 0:n])
                s(last, "oT")
                if n == NS:
                    for h in range(H):
                        pe.wait_ge(S("gs_vm"), h + 1)
                        if h:
                            pe.wait_ge(S("gs_new"), h)
                        for q in range(2):
                            last = mm(B[q][:, :], m["KD"][0:n, h, :],
                                      m["VNM"][0:n, 4 * q:4 * q + 4, :])
                        last.then_inc(S("gs_ds"), 1)

            def ml_prep():
                pe.wait_ge(S("mg_ready"), 1)
                for part, b0 in ((0, 0), (1, 3)):
                    for t in range(TILES + 1):
                        n = P if t < TILES else NS
                        last = pe.transpose(B[b0 + t // 4][0:H, (t % 4) * P:(t % 4) * P + n],
                                            cols[0:n, t, part, :], ident[0:n, 0:n])
                last.then_inc(S("m_rows"), 1)
                pe.wait_ge(S("m_rows_done"), 1)
                pe.wait_ge(S("m_lw_done"), 1)
                for t in range(TILES + 1):
                    n = P if t < TILES else NS
                    for q, r in enumerate((AR, LWR, MR)):
                        last = pe.transpose(B[6][0:n, t * 12 + 4 * q:t * 12 + 4 * q + 4],
                                            r[0:H, t * P:t * P + n], ident[0:H, 0:H])
                last.then_inc(S("m_cols"), 1)
                for h in range(H):
                    last = mm(B[7][:, h * 2 * NB:(h + 1) * 2 * NB], sel[:, h, :], KPR[0:H, :])
                last.then_inc(S("m_keep"), 1)

            def ml(t, n):
                m = ml_map(n)
                X = m["X"]
                w = lambda name, v=None: pe.wait_ge(S("g_" + name), t + (1 + TILES + 1) if v is None else v)
                s = lambda ins, name: ins.then_inc(S("g_" + name), 1)
                w("gr")
                for h in range(H):
                    last = mm(B4(0)[0:n, h, 0:n], sel[:, h, 0:n], rows4[:, 0, 0:n])
                s(last, "bc")
                for h in range(H):
                    last = mm(B4(1)[:, h, 0:n], sel[:, h, :], rows4[:, 1, 0:n])
                s(last, "bcW")
                pe.wait_ge(S("g_xin"), (t + (TILES + 2)) * 16)
                for h in range(H):
                    last = mm(B4(2)[0:n, h, 0:n], X[:, 4 + h, :], X[:, h, :])
                s(last, "kq")
                for h in range(H):
                    last = pe.transpose(B4(3)[0:n, h, :], X[:, 4 + h, :], ident[:, :])
                s(last, "kT")
                for c in range(8):
                    last = pe.transpose(B4(4 + c // 4)[0:n, c % 4, :], X[:, 8 + c, :], ident[:, :])
                s(last, "vT")
                w("vb")
                w("qk")
                w("qd")
                w("DTe")
                w("E")
                for h in range(H):
                    bank = B[(0, 1, 6, 7)[h]]
                    if n == P:
                        w("state")
                        mm(bank[0:n, 0:DV + 1], m["QD"][:, h, :], CN[:, h, :], start=True, stop=False)
                    else:
                        pe.wait_ge(S(f"ms_cin{h % 2}"), 32 * (h // 2 + 1))
                        for b in range(NB):
                            mm(bank[0:n, 0:DV + 1], m["QDM"][:, h, b, :], m["CS2"][:, h % 2, b, :],
                               start=b == 0, stop=False)
                    last = mm(bank[0:n, 0:DV + 1], m["ST"][0:n, h, :], m["V1"][0:n, h, :],
                              start=False, stop=True)
                    if n == NS:
                        last.then_inc(S("ms_num"), 1)
                        pe.wait_ge(S("ms_vm"), h + 1)
                        w("rhs")
                        for b in range(NB):
                            if h * NB + b >= 4:
                                pe.wait_ge(S("ms_upd"), h * NB + b - 3)
                            mm(B[2 + b % 4][:, 0:DV + 1], m["KW"][0:n, h, :], m["VM"][0:n, b, :])\
                                .then_inc(S("ms_dc"), 1)
                if n == P:
                    s(last, "num")
                    w("rhs")
                    for h in range(H):
                        last = mm(B[2 + h][:, 0:DV + 1], m["KW"][:, h, :], m["V1"][:, h, :])
                    s(last, "ds")
                w("on")
                if n == P:
                    w("state", t + (TILES + 3))
                for half in range(2):
                    for h in range(H):
                        last = pe.transpose(B4(4 + half)[:, h, 0:n], m["HN"][0:n, h, half * P:(half + 1) * P],
                                            ident[0:n, 0:n])
                    s(last, ("z", "oT")[half])

            def store_y():
                pe.wait_ge(S("x_ready"), 4 * KT)
                for t in range(TILES + 1):
                    n = P if t < TILES else NS
                    for q in range(2):
                        b = (2 * t + q) % 4
                        if 2 * t + q >= 4:
                            pe.wait_ge(S("y_copied"), 2 * t + q - 3)
                        for c in range(4):
                            last = pe.transpose(B[b][0:n, c * P:(c + 1) * P], xT[:, 4 * q + c, t * P:t * P + n],
                                                ident[:, :])
                        last.then_inc(S("x_turned"), 1)

            load_x()
            for l in range(2):
                phase_end(pe, "pe")
                norm(4 * l)
                gate_cols(l)
                if l == 0:
                    for c in range(NCONV):
                        if c == 0:
                            pe.wait_ge(S("wg_loaded"), 32)
                        last = pe.transpose(B[7][:, c * 24:(c + 1) * 24], cs_tm[0:24, c * P:(c + 1) * P],
                                            ident[0:24, 0:24])
                    last.then_inc(S("cs_T"), 1)
                linear(U0[l], AE0[l], NCH // 2)
                if l == 0:
                    conv_tails()
                phase_end(pe, "pe")
                if l == 0:
                    gdn_prep()
                    phase_end(pe, "pe")
                    with pe.Fori(0, TILES) as t:
                        gdn(t, P, LEVELS, t * LEVELS)
                        pe.drain().then_inc(S("g_tile"), 1)
                    phase_end(pe, "pe")
                    gdn(TILES, NS, LEVELS_S, TILES * LEVELS)
                else:
                    ml_prep()
                    phase_end(pe, "pe")
                    with pe.Fori(0, TILES) as t:
                        ml(t, P)
                        pe.drain().then_inc(S("g_tile"), 1)
                    phase_end(pe, "pe")
                    ml(TILES, NS)
                phase_end(pe, "pe")
                linear(U0[l] + U_IN, AE0[l] + J_IN, KT // 2)
                norm(4 * l + 1)
                norm(4 * l + 2)
                phase_end(pe, "pe")
                ff(l)
                phase_end(pe, "pe")
                norm(4 * l + 3)
            phase_end(pe, "pe")
            store_y()

        @block.scalar
        def _(act):
            A_ = act.activation

            def hi(u, k):
                act.wait_ge(S("w_used"), u + 1)
                act.wait_ge(S(f"w_loaded{k % 2}"), 8 * u + (16 - 8 * (k % 2)))
                A_(whi[:, k % 2, :], wst[:, k % 2, :], ACT.Copy).then_inc(S("w_hi"), 1)

            def norm_sq(nn, src, ready):
                for c in range(KT):
                    ready(c)
                    if c >= 2:
                        act.wait_ge(S("squares_added"), KT * nn + c - 1)
                    A_(sq2[:, c % 2], src[:, c], ACT.Square).then_inc(S("squared"), 1)
                act.wait_ge(S("sumsq"), nn + 1)
                for tg in range(TG):
                    A_(lnss[:, tg * N:(tg + 1) * N], B[tg][:, 0:N], ACT.Ln, bias=epsc[:, :],
                       scale=1.0 / D).then_inc(S("lnss"), 1)
                act.wait_ge(S("lnss"), TG * (nn + 1))
                A_(rstd[:, :], lnss[:, :], ACT.Exp, scale=-0.5).then_inc(S("rstd"), 1)

            def norm_hi(m):
                for c in range(KT):
                    act.wait_ge(S("h_full"), KT * m + c + 1)
                    A_(hhi[:, c], hf2[:, c % 2], ACT.Copy).then_inc(S("h_hi"), 1)

            def x_ready(l_posts):
                return lambda c: act.wait_ge(S("x_ready"), KT * (l_posts - 1) + c + 1) if l_posts else None

            def load_x():
                act.sem_inc(S("act_evac"), BANKS)
                act.wait_ge(S("par_T"), 1)
                A_(par[:, :], B[6][:, 0:P], ACT.Copy).then_inc(S("par_ready"), 1)

            def plain_unit(j0, c_par, u, k, s0, func, nb):
                act.wait_ge(S("row_free"), s0)
                for tg in range(TG):
                    act.wait_ge(S("job_done"), j0 + tg + 1)
                    A_(pout2[:, k % 2, tg * N:(tg + 1) * N], B[(k % 2) * TG + tg][:, 0:N], func)\
                        .then_inc(S("act_evac"), 1)

            def in_proj(l):
                u0, j0 = U0[l], J0[l]
                hi(u0, 0) if l == 0 else None

                def evac(i, c0, k, func):
                    plain_unit(i * 6 + (j0 + (c0 + k) * TG), None, None, k,
                               i * 2 + (l * NCH + c0 + k + 1), func, None)

                def conv(i, k):
                    j = i * 6 + (j0 + k * TG)
                    act.wait_ge(S("tails_ready"), i * 2 + (k + 1))
                    row = xc2[:, k]
                    for tg in range(TG):
                        act.wait_ge(S("job_done"), j + tg + 1)
                        b = B[k * TG + tg]
                        if tg < TG - 1:
                            A_(row[:, 3 + tg * N:3 + (tg + 1) * N], b[:, 0:N], ACT.Copy).then_inc(S("act_evac"), 1)
                        else:
                            r = NP - tg * N
                            A_(row[:, 3 + tg * N:3 + NP], b[:, 0:r], ACT.Copy)
                            A_(row[:, XC:XCW].rearrange("p (b s) -> p b s", b=NB)[:, :, 3:3 + LS],
                               b[:, r:N].rearrange("p (b s) -> p b s", b=NB), ACT.Copy)\
                                .then_inc(S("act_evac"), 1)
                    act.wait_ge(S("conv_done"), i * 2 + (k + 1))
                    act.wait_ge(S("row_free"), i * 2 + (k + 1))
                    A_(pout2[:, k], cy2[:, k], ACT.Silu).then_inc(S("conv_act"), 1)

                spans = [(0, 6, "conv"), (12, 2, ACT.Silu), (16, 4, ACT.Gelu)] if l == 0 else \
                    [(0, 8, ACT.Copy), (16, 4, ACT.Sigmoid)]
                for c0, iters, func in spans:
                    with act.Fori(0, iters) as i:
                        for k in range(2):
                            hi(i * 2 + (u0 + c0 + k + 1), (k + 1) % 2)
                            if func == "conv":
                                conv(i, k)
                            else:
                                evac(i, c0, k, func)

            def out_proj(l):
                u0, j0 = U0[l] + U_IN, J0[l] + J_IN
                with act.Fori(0, KT // 2) as i:
                    for k in range(2):
                        hi(i * 2 + (u0 + k + 1), (k + 1) % 2)
                        for tg in range(TG):
                            act.wait_ge(S("job_done"), i * 6 + (j0 + k * TG + tg + 1))
                            A_(accd(i * 2 + k, tg), B[k * TG + tg][:, 0:N].unsqueeze(1), ACT.Copy).then_inc(S("act_evac"), 1)

            def ff_group(l, g, last):
                u0 = U0[l] + U_IN + U_OUT
                j0 = J0[l] + J_IN + J_OUT
                q0 = l * FG * J_W1
                for k in range(FK):
                    hi(g * (2 * FK) + (u0 + k + 1), (k + 1) % 2)
                    for tg in range(TG):
                        j = k * TG + tg
                        act.wait_ge(S("job_done"), g * (J_W1 + J_W2) + (j0 + j + 1))
                        act.wait_ge(S("h1_split"), g * J_W1 + (q0 + j + 1))
                        A_(relu2[:, j % 2], B[j % BANKS][:, 0:N], ACT.Relu).then_inc(S("act_evac"), 1)
                        act.wait_ge(S("act_evac"), g * J_W1 + (AE0[l] + J_IN + J_OUT + BANKS + j + 1))
                        A_(h1hi[:, k, tg * N:(tg + 1) * N], relu2[:, j % 2], ACT.Square)\
                            .then_inc(S("h1_hi"), 1)
                for k in range(FK):
                    if not (last and k == FK - 1):
                        hi(g * (2 * FK) + (u0 + FK + k + 1), (k + 1) % 2)

            def gdn_prep():
                act.wait_ge(S("gates_sb"), 1)
                gv = gates[:, :, :]
                A_(cols[:, :, 1, :], gv[:, :, 0:4], ACT.Sigmoid).then_inc(S("gexp"), 1)
                act.wait_ge(S("hvec_loaded"), 32)
                A_(hvec[:, 2, :], hvec[:, 0, :], ACT.Exp).then_inc(S("gexp"), 1)
                act.wait_ge(S("z_ready"), 1)
                z = gtmp[:, 0, :]
                A_(gtmp[:, 1, :], z, ACT.Abs).then_inc(S("gp"), 1)
                act.wait_ge(S("gp"), 1)
                A_(gtmp[:, 2, :], gtmp[:, 1, :], ACT.Exp, scale=-1.0).then_inc(S("gp"), 1)
                act.wait_ge(S("gp"), 2)
                A_(gtmp[:, 1, :], gtmp[:, 2, :], ACT.Ln, bias=1.0).then_inc(S("gp"), 1)
                act.wait_ge(S("gc_ready"), 1)
                A_(cols[:, :, 2, :], cols[:, :, 0, :], ACT.Exp).then_inc(S("gexp"), 1)
                act.wait_ge(S("kd_ready"), 1)
                A_(cols[:, :, 3, :], cols[:, :, 3, :], ACT.Exp).then_inc(S("gexp"), 1)
                A_(cols[:, 0:TILES, 4, :], B[7][:, 36:68].rearrange("p (t h) -> p t h", h=H), ACT.Exp)\
                    .then_inc(S("gexp"), 1)
                A_(keepb[:, 0:2, :].rearrange("p a b -> p (a b)"), B[7][:, 72:104], ACT.Exp)\
                    .then_inc(S("gexp"), 1)
                act.wait_ge(S("gc_rows"), 1)
                for q in range(2):
                    A_(GR[0:H, q * 512:(q + 1) * 512], B[q][0:H, :], ACT.Copy)
                A_(GR[0:H, NP:T], B[2][0:H, 0:NS], ACT.Copy)

            def rms_cols(s, w, src, ssq, lnv, out, width, n, chain):
                w(chain)
                s(A_(lnv, ssq, ACT.Ln, bias=epsc[0:n, :], scale=1.0 / width), chain + "l")
                w(chain + "l")
                s(A_(out, lnv, ACT.Exp, scale=-0.5), chain + "r")

            def gdn(t, n):
                m = gdn_map(n)
                X = m["X"]
                w = lambda name, v=None: act.wait_ge(S("g_" + name), t + 1 if v is None else v)
                s = lambda ins, name: ins.then_inc(S("g_" + name), 1)
                s(A_(rows4[:, 0, 0:n], GR[0:H, bass.ds(t * P, n)], ACT.Copy), "gr")
                act.wait_ge(S("g_xin"), (t + 1) * 16)
                s(A_(m["SQ"], X[:, 0:8, :], ACT.Square), "sq")
                w("vsT")
                for g in range(H):
                    last = A_(m["VB"][0:n, g, :], B4(7)[0:n, g, :], ACT.Square, accum_out=small[0:n, 0, g:g + 1])
                s(last, "vss")
                rms_cols(s, w, None, small[0:n, 0, :], small[0:n, 1, :], small[0:n, 2, :], P, n, "vss")
                w("ss")
                A_(m["RB"][:, 0:4], B4(0)[:, :, 0:n], ACT.Ln, bias=epsc[:, :])
                s(A_(m["RB"][:, 4:8], B4(1)[:, :, 0:n], ACT.Ln, bias=epsc[:, :]), "ln")
                w("ln")
                s(A_(m["RB"], m["RB"], ACT.Exp, scale=-0.5), "rb")
                w("bc")
                s(A_(m["E"], B4(2)[:, :, 0:n], ACT.Exp), "E")
                w("du")
                s(A_(m["Dm"][0:n], m["Dm"][0:n], ACT.Exp, scale=-1.0), "D")
                w("dtu")
                s(A_(m["DT"][0:n], m["DT"][0:n], ACT.Exp), "DTe")
                w("w")
                w("qn")
                s(A_(m["NW"], B4(3)[:, :, 0:n], ACT.Copy, scale=-1.0), "nw" if n == P else "nws")
                w("vnew")
                s(A_(m["VN"][0:n], B4(4)[0:n], ACT.Copy), "vns")
                w("o")
                for h in range(H):
                    last = A_(m["ON"][0:n, h, :], B4(5)[0:n, h, :], ACT.Square, accum_out=small[0:n, 3, h:h + 1])
                s(last, "oss")
                rms_cols(s, w, None, small[0:n, 3, :], small[0:n, 4, :], small[0:n, 5, :], P, n, "oss")
                w("ofa")
                w("ofb")
                s(A_(hhi[:, :, bass.ds(t * P, n)], m["OF"], ACT.Copy), "hi")

            def ml_prep():
                act.wait_ge(S("mz_ready"), 1)
                z = gtmp[:, 0, :]
                A_(gtmp[:, 1, :], z, ACT.Abs).then_inc(S("mp"), 1)
                act.wait_ge(S("mp"), 1)
                A_(gtmp[:, 2, :], gtmp[:, 1, :], ACT.Exp, scale=-1.0).then_inc(S("mp"), 1)
                act.wait_ge(S("mp"), 2)
                A_(gtmp[:, 1, :], gtmp[:, 2, :], ACT.Ln, bias=1.0).then_inc(S("mp"), 1)
                act.wait_ge(S("m_rows"), 1)
                for b0, dst in ((0, IR), (3, LF)):
                    for q in range(2):
                        A_(dst[0:H, q * 512:(q + 1) * 512], B[b0 + q][0:H, :], ACT.Copy)
                    A_(dst[0:H, NP:T], B[b0 + 2][0:H, 0:NS], ACT.Copy).then_inc(S("m_rows_sb"), 1)
                act.wait_ge(S("m_keep_in"), 1)
                A_(KPR[0:H, :], KPR[0:H, :], ACT.Exp).then_inc(S("m_rows_done"), 1)
                act.wait_ge(S("m_cols"), 1)
                for q, (lo_, func, sc) in enumerate(((0, ACT.Copy, 1.0), (4, ACT.Exp, 1.0), (8, ACT.Exp, -1.0))):
                    A_(cum[:, 0:TILES, lo_:lo_ + 4],
                       B[6][:, 0:96].rearrange("p (t c) -> p t c", c=12)[:, :, lo_:lo_ + 4], func, scale=sc)
                    A_(cum[0:NS, TILES, lo_:lo_ + 4], B[6][0:NS, 96 + lo_:100 + lo_], func, scale=sc)
                act.wait_ge(S("m_keep"), 1)
                A_(keepb[:, :, :].rearrange("p a b -> p (a b)"), B[7][:, 0:H * 2 * NB], ACT.Copy)

            def ml(t, n):
                m = ml_map(n)
                w = lambda name, v=None: act.wait_ge(S("g_" + name), t + (1 + TILES + 1) if v is None else v)
                s = lambda ins, name: ins.then_inc(S("g_" + name), 1)
                A_(rows4[:, 0, 0:n], ROWM[0:H, bass.ds(t * P, n)], ACT.Copy)
                s(A_(rows4[:, 1, 0:n], ROWW[0:H, bass.ds(t * P, n)], ACT.Copy), "gr")
                w("bcW", t + 1)
                s(A_(m["E"], B4(1)[:, :, 0:n], ACT.Exp), "E")
                w("dtu")
                s(A_(m["WTm"][0:n], m["WTm"][0:n], ACT.Exp), "DTe")
                w("vT")
                for q in range(2):
                    last = A_(m["V1"][0:n, 2 * q:2 * q + 2, 0:DV],
                              B[4 + q][0:n, :].rearrange("p (h v) -> p h v", h=2), ACT.Copy)
                s(last, "vb")
                for h in range(H):
                    act.wait_ge(S("ms_num"), h + 1) if n == NS else (w("num", t + 1) if h == 0 else None)
                    bank = B[(0, 1, 6, 7)[h]]
                    A_(small[0:n, 1, h:h + 1], bank[0:n, DV:DV + 1], ACT.Abs)
                    last = A_(m["HN"][0:n, h], bank[0:n, 0:DV], ACT.Square, accum_out=small[0:n, 0, h:h + 1])
                s(last, "oss")
                w("ms", t + 1)
                s(A_(small[0:n, 4, :], small[0:n, 3, :], ACT.Ln, bias=epsc[0:n, :], scale=1.0 / DV), "ossl")
                w("ossl")
                s(A_(small[0:n, 5, :], small[0:n, 4, :], ACT.Exp, scale=-0.5), "ossr")
                w("ofa")
                w("ofb")
                s(A_(hhi[:, :, bass.ds(t * P, n)], m["OF"], ACT.Copy), "hi")

            def store_y():
                for t in range(TILES + 1):
                    n = P if t < TILES else NS
                    for q in range(2):
                        act.wait_ge(S("x_turned"), 2 * (TILES + 1) + 2 * t + q + 1)
                        if t >= 2:
                            act.wait_ge(S(f"y_stored{t % 2}"), 16 * (t // 2))
                        A_(x_tm[0:n, t % 2, q * 512:(q + 1) * 512], B[(2 * t + q) % 4][0:n, :], ACT.Copy)\
                            .then_inc(S("y_copied"), 1)

            load_x()
            phase = lambda: phase_end(act, "act")
            for l in range(2):
                phase()
                norm_sq(4 * l, xT, x_ready(2 * l))
                norm_hi(2 * l)
                if l == 0:
                    act.wait_ge(S("cs_T"), 1)
                    A_(csT.rearrange("p a b -> p (a b)"), B[7][:, 0:NCONV * 24], ACT.Copy).then_inc(S("csT_ready"), 1)
                act.wait_ge(S("gates_done"), l + 1)
                if l == 0:
                    act.wait_ge(S("cols_zero"), 1)
                A_(gates[:, 0:TILES, :], B[6][:, 0:64].rearrange("p (t c) -> p t c", c=8), ACT.Copy)
                A_(gates[0:NS, TILES, :], B[6][0:NS, 64:72], ACT.Copy).then_inc(S("gates_sb"), 1)
                in_proj(l)
                if l == 0:
                    act.wait_ge(S("tails_T"), 1)
                    for q in range(3):
                        last = A_(tail_tm[0:27, q * 512:(q + 1) * 512], B[q][0:27, :], ACT.Copy)
                    last.then_inc(S("tails_sb"), 1)
                phase()
                if l == 0:
                    gdn_prep()
                    phase()
                    with act.Fori(0, TILES) as t:
                        act.wait_ge(S("g_tile"), t * 3 + 3)
                        gdn(t, P)
                        act.drain().then_inc(S("g_tile"), 1)
                    phase()
                    gdn(TILES, NS)
                else:
                    ml_prep()
                    phase()
                    with act.Fori(0, TILES) as t:
                        act.wait_ge(S("g_tile"), t * 3 + 3 * (TILES + 1))
                        ml(t, P)
                        act.drain().then_inc(S("g_tile"), 1)
                    phase()
                    ml(TILES, NS)
                phase()
                out_proj(l)
                act.wait_ge(S("act_evac"), BANKS + AE0[l] + J_IN + J_OUT)
                norm_sq(4 * l + 1, acc, lambda c: None)
                norm_sq(4 * l + 2, xT, x_ready(2 * l + 1))
                norm_hi(2 * l + 1)
                phase()
                with act.Fori(0, FG - 1) as g:
                    ff_group(l, g, False)
                ff_group(l, FG - 1, l == 1)
                phase()
                norm_sq(4 * l + 3, acc, lambda c: None)
            phase()
            store_y()

        @block.vector
        def _(dve):
            def lo(u, k):
                dve.wait_ge(S("w_hi"), u + 1)
                dve.tensor_tensor(wlo[:, k % 2, :], wst[:, k % 2, :], whi[:, k % 2, :].bitcast(F32),
                                  ALU.subtract).then_inc(S("w_split"), 1)

            def add_squares(nn):
                for c in range(KT):
                    dve.wait_ge(S("squared"), KT * nn + c + 1)
                    if c == 0:
                        ins = dve.tensor_copy(ssum[:, :], sq2[:, 0])
                    else:
                        dve.wait_ge(S("squares_added"), KT * nn + c)
                        ins = dve.tensor_tensor(ssum[:, :], ssum[:, :], sq2[:, c % 2], ALU.add)
                    ins.then_inc(S("squares_added"), 1)

            def gain(l, q, c):
                return par[:, (l * 4 + q) * KT + c:(l * 4 + q) * KT + c + 1]

            def pre_norm(nn, m):
                add_squares(nn)
                l, q = nn // 4, nn % 4
                dve.wait_ge(S("rstd"), nn + 1)
                dve.wait_ge(S("par_ready"), 1)

                def rest(c):
                    dve.wait_ge(S("h_hi"), KT * m + c + 1)
                    dve.tensor_tensor(hlo[:, c], hf2[:, c % 2], hhi[:, c].bitcast(F32), ALU.subtract)\
                        .then_inc(S("h_split"), 1)
                for c in range(KT):
                    if c >= 2:
                        dve.wait_ge(S("h_split"), KT * m + c - 1)
                    dve.scalar_tensor_tensor(hf2[:, c % 2], xT[:, c], gain(l, q, c), rstd[:, :], ALU.mult,
                                             ALU.mult).then_inc(S("h_full"), 1)
                    if c:
                        rest(c - 1)
                rest(KT - 1)

            def post_norm(nn):
                add_squares(nn)
                l, q = nn // 4, nn % 4
                p = nn // 2
                dve.wait_ge(S("rstd"), nn + 1)
                for c in range(KT):
                    if c >= 2:
                        dve.wait_ge(S("x_ready"), KT * p + c - 1)
                    dve.scalar_tensor_tensor(hf2[:, c % 2], acc[:, c], gain(l, q, c), rstd[:, :], ALU.mult,
                                             ALU.mult).then_inc(S("mix_normed"), 1)

            def load_x():
                dve.sem_inc(S("dve_evac"), BANKS)
                dve.sem_inc(S("w_split"), 2)
                dve.sem_inc(S("tails_ready"), 2)
                dve.sem_inc(S("h1_split"), 2)
                dve.sem_inc(S("xT_copied"), 4)
                dve.memset(epsc[:, :], EPS)
                with dve.Fori(0, TILES // 2) as i:
                    for k in range(2):
                        for q in range(2):
                            dve.wait_ge(S("x_turned"), i * 4 + (2 * k + q + 1))
                            dve.tensor_copy(xT[:, 4 * q:4 * q + 4, bass.ds(i * (2 * P) + k * P, P)],
                                            B4(2 * k + q)).then_inc(S("xT_copied"), 1)
                for q in range(2):
                    dve.wait_ge(S("x_turned"), 2 * TILES + q + 1)
                    dve.tensor_copy(xT[:, 4 * q:4 * q + 4, NP:T],
                                    B[q][:, 0:4 * NS].rearrange("p (c n) -> p c n", c=4)).then_inc(S("xT_copied"), 1)

            def conv_block(i, k):
                cw = cw2[:, k]
                c = i * 2 + k
                dve.tensor_copy(cw[:, :].unsqueeze(2), par[:, bass.ds(64 + c, 3 * NCONV + 1, 1)][:, 0:37:NCONV]
                                .unsqueeze(2)) if False else None
                for j in range(CONVW):
                    last = dve.tensor_copy(cw[:, j:j + 1], par[:, bass.ds(c + (64 + j * NCONV), 1)])
                row, y = xc2[:, k], cy2[:, k]
                smp = row[:, XC:XCW].rearrange("p (b s) -> p b s", b=NB)
                dve.tensor_copy(smp[:, :, 0:3], csT[:, bass.ds(c, 1), :].rearrange("p a (b s) -> p (a b) s", s=3))\
                    .then_inc(S("taps"), 1)
                dve.wait_ge(S("taps"), i * 2 + (k + 1))
                dve.wait_ge(S("act_evac"), i * 6 + (BANKS + (k + 1) * TG))
                dve.wait_ge(S("conv_act"), i * 2 + (k + 1))
                ys = y[:, NP:T].rearrange("p (b s) -> p b s", b=NB)
                for j in range(CONVW):
                    parts = ((y[:, 0:NP], row[:, j:j + NP]), (ys, smp[:, :, j:j + LS]))
                    if j:
                        dve.wait_ge(S("tap"), i * 8 + (4 * k + j))
                    for o, x in parts:
                        if j == 0:
                            ins = dve.tensor_scalar(o, x, cw[:, 0:1], None, ALU.mult)
                        else:
                            ins = dve.scalar_tensor_tensor(o, x, cw[:, j:j + 1], o, ALU.mult, ALU.add)
                    ins.then_inc(S("tap"), 1)
                dve.wait_ge(S("tap"), i * 8 + (4 * k + 4))
                dve.tensor_copy(tails[:, bass.ds(c, 1), 0:3], row[:, NP:NP + 3].unsqueeze(1))\
                    .then_inc(S("conv_done"), 1)
                dve.tensor_copy(tails[:, bass.ds(c, 1), 3:27].rearrange("p a (b s) -> p (a b) s", s=3),
                                smp[:, :, LS:LS + 3]).then_inc(S("tails_ready"), 1)

            def in_proj(l):
                u0 = U0[l]
                if l == 0:
                    dve.memset(xc2[:, :, 0:3], 0.0)
                    dve.wait_ge(S("csT_ready"), 1)
                    lo(0, 0)
                    with dve.Fori(0, 6) as i:
                        for k in range(2):
                            lo(i * 2 + (k + 1), (k + 1) % 2)
                            conv_block(i, k)
                    with dve.Fori(0, 6) as i:
                        for k in range(2):
                            lo(i * 2 + (12 + k + 1), (k + 1) % 2)
                else:
                    with dve.Fori(0, NCH // 2) as i:
                        for k in range(2):
                            lo(i * 2 + (u0 + k + 1), (k + 1) % 2)

            def ff_group(l, g, last):
                u0 = U0[l] + U_IN + U_OUT
                j0 = J0[l] + J_IN + J_OUT
                q0 = l * FG * J_W1
                for k in range(FK):
                    lo(g * (2 * FK) + (u0 + k + 1), (k + 1) % 2)
                    for tg in range(TG):
                        j = k * TG + tg
                        dve.wait_ge(S("h1_hi"), g * J_W1 + (q0 + j + 1))
                        dve.tensor_tensor(relu2[:, j % 2], relu2[:, j % 2], relu2[:, j % 2], ALU.mult)\
                            .then_inc(S("h1_sq"), 1)
                        dve.wait_ge(S("h1_sq"), g * J_W1 + (q0 + j + 1))
                        dve.tensor_tensor(h1lo[:, k, tg * N:(tg + 1) * N], relu2[:, j % 2],
                                          h1hi[:, k, tg * N:(tg + 1) * N].bitcast(F32), ALU.subtract)\
                            .then_inc(S("h1_split"), 1)
                for k in range(FK):
                    if not (last and k == FK - 1):
                        lo(g * (2 * FK) + (u0 + FK + k + 1), (k + 1) % 2)
                    for oc in range(2):
                        for tg in range(TG):
                            j = (2 * k + oc) * TG + tg
                            a = acc[:, 2 * k + oc, tg * N:(tg + 1) * N]
                            dve.wait_ge(S("job_done"), g * (J_W1 + J_W2) + (j0 + J_W1 + j + 1))
                            dve.tensor_tensor(a, B[j % BANKS][:, 0:N], a, ALU.add).then_inc(S("dve_evac"), 1)

            def bcl(ap, shape):
                return ap.unsqueeze(2).broadcast_to(shape)

            def bcm(ap, shape):
                return ap.unsqueeze(1).broadcast_to(shape)

            TT, STT = dve.tensor_tensor, dve.scalar_tensor_tensor

            def gdn_prep():
                dve.wait_ge(S("gates_sb"), 1)
                dve.wait_ge(S("hvec_loaded"), 32)
                z = gtmp[:, 0, :].rearrange("p (t h) -> p t h", h=H)
                TT(z, gates[:, :, 4:8], bcm(hvec[:, 1, :], [P, TILES + 1, H]), ALU.add).then_inc(S("z_ready"), 1)
                dve.wait_ge(S("gp"), 3)
                STT(gtmp[:, 2, :], gtmp[:, 0, :], 0.0, gtmp[:, 1, :], ALU.max, ALU.add).then_inc(S("gq"), 1)
                dve.wait_ge(S("gq"), 1)
                dve.wait_ge(S("gexp"), 2)
                STT(cols[:, :, 5, :], gtmp[:, 2, :].rearrange("p (t h) -> p t h", h=H), -1.0,
                    bcm(hvec[:, 2, :], [P, TILES + 1, H]), ALU.mult, ALU.mult).then_inc(S("cols_g"), 1)
                dve.wait_ge(S("cols_g"), 1)
                TT(gtmp[0:NS, 3, 0:32].rearrange("p (b h) -> p b h", h=H), bcm(cols[0:NS, TILES, 5, :], [NS, NB, H]),
                   bcl(rowmask[:, :], [NS, NB, H]), ALU.mult).then_inc(S("gmask_ready"), 1)
                dve.wait_ge(S("cum_done"), 1)
                dve.wait_ge(S("cols_zero"), 1)
                dve.tensor_copy(cols[:, 0:TILES, 0, :], B[7][:, 0:32].rearrange("p (t h) -> p t h", h=H))
                dve.tensor_copy(cols[0:NS, TILES, 0, :], B[7][0:NS, 32:36]).then_inc(S("gc_ready"), 1)
                dve.wait_ge(S("gc_ready"), 1)
                TT(cols[:, 0:TILES, 3, :], B[7][:, 36:68].rearrange("p (t h) -> p t h", h=H),
                   cols[:, 0:TILES, 0, :], ALU.subtract)
                TT(cols[0:NS, TILES, 3, :], B[7][0:NS, 68:72], cols[0:NS, TILES, 0, :], ALU.subtract)\
                    .then_inc(S("kd_ready"), 1)
                dve.wait_ge(S("gexp"), 6)
                TT(cols[:, :, 2, :], cols[:, :, 2, :], cols[:, :, 1, :], ALU.mult)
                dve.wait_ge(S("sgw_T"), 1)
                TT(WT[:, :, :], B4(3), bcm(triU[:, :], [P, H, P]), ALU.mult)
                TT(WTS[0:NS], B[4][0:NS, 0:H * NS].rearrange("p (g n) -> p g n", g=H), bcm(triUS[:, :], [NS, H, NS]), ALU.mult)
                dve.memset(St[:, :, :], 0.0).then_inc(S("g_state"), 1)

            def gdn(t, n, lv, lv0):
                m = gdn_map(n)
                X, QH = m["X"], m["QH"]
                w = lambda name, v=None: dve.wait_ge(S("g_" + name), t + 1 if v is None else v)
                s = lambda ins, name: ins.then_inc(S("g_" + name), 1)
                s(dve.tensor_copy(tcol[0:n].unsqueeze(1), cols[0:n, bass.ds(t, 1)]), "tc")
                gc, beta, begc, kdec, gl = (tcol[0:n, i, :] for i in range(5))
                w("tc")
                w("vssr")
                s(TT(m["VB"][0:n], B4(7)[0:n], bcl(small[0:n, 2, :], [n, H, P]), ALU.mult), "vbr")
                w("vbr")
                s(TT(m["VB"][0:n], m["VB"][0:n], GSG[0:n], ALU.mult), "vb")
                w("rb")
                s(TT(QH[:, 4:8], X[:, 4:8], m["RB"][:, 4:8], ALU.mult), "kn")
                s(STT(QH[:, 0:4], X[:, 0:4], QSCALE, m["RB"][:, 0:4], ALU.mult, ALU.mult), "qn")
                w("E")
                mp, mn = (maskpos, masknegT) if n == P else (maskposS, masknegTS)
                for h in range(H):
                    last = STT(m["Dm"][0:n, h], B4(2)[0:n, h, 0:n], gc[:, h:h + 1], mp[:, :], ALU.subtract, ALU.add)
                s(last, "du")
                for h in range(H):
                    last = STT(m["DT"][0:n, h], B4(2)[0:n, h, 0:n], gc[:, h:h + 1], mn[:, :], ALU.subtract, ALU.add)
                s(last, "dtu")
                w("qn")
                s(TT(m["QD"], QH[:, 0:4], m["E"], ALU.mult), "qd" if n == P else "qds")
                if n == NS:
                    w("qds", 1)
                    s(TT(m["QDM"], m["QD"].unsqueeze(2).broadcast_to([P, H, NB, NS]),
                         colmask[:, :, :].unsqueeze(1).broadcast_to([P, H, NB, NS]), ALU.mult), "qd")
                w("D")
                w("kk")
                for h in range(H):
                    last = STT(m["A"][0:n, h], B4(3)[0:n, h, 0:n], beta[:, h:h + 1], m["Dm"][0:n, h],
                               ALU.mult, ALU.mult)
                s(last, "A")
                w("DTe")
                w("kq")
                s(TT(m["DT"][0:n], B4(4)[0:n, :, 0:n], m["DT"][0:n], ALU.mult), "qk")
                dve.tensor_copy(m["Xi"][0:n], bcm(ident[0:n, 0:n], [n, H, n]))
                s(dve.tensor_copy(m["XiT"][0:n], bcm(ident[0:n, 0:n], [n, H, n])), "Xinit")
                w("kT")
                w("vT")
                TT(m["RW"][0:n], B4(5)[0:n], bcl(begc, [n, H, P]), ALU.mult)
                TT(m["KD"][0:n], B4(5)[0:n], bcl(kdec, [n, H, P]), ALU.mult)
                s(TT(m["RU"][0:n], B4(6)[0:n], bcl(beta, [n, H, P]), ALU.mult), "rhs")
                w("z")
                s(TT(m["OF"][:, 4:8], B4(3)[:, :, 0:n], X[:, 16:20], ALU.mult), "ofb")
                for q in range(lv):
                    w("t2", lv0 + q + 1)
                    s(TT(m["T2"][0:n], B4(0)[0:n, :, 0:n], bcm(lmask[0:n, q, 0:n], [n, H, n]), ALU.mult), "t2s")
                    w("x1", lv0 + q + 1)
                    w("x2", lv0 + q + 1)
                    TT(m["Xi"][0:n], m["Xi"][0:n], B4(1)[0:n, :, 0:n], ALU.subtract)
                    s(TT(m["XiT"][0:n], m["XiT"][0:n], B4(2)[0:n, :, 0:n], ALU.subtract), "inv")
                    w("inv", lv0 + q + 1)
                if n == NS:
                    w("nws", 1)
                    s(TT(m["NWM"], m["NW"].unsqueeze(2).broadcast_to([P, H, NB, NS]),
                         colmask[:, :, :].unsqueeze(1).broadcast_to([P, H, NB, NS]), ALU.mult), "nw")
                w("o")
                if n == P:
                    s(TT(St[:, :, :], St[:, :, :], bcl(gl, [P, H, P]), ALU.mult), "sg")
                    w("sg")
                    w("ds")
                    s(TT(St[:, :, :], St[:, :, :], B4(6), ALU.add), "state")
                w("ossr")
                s(TT(m["ON"][0:n], B4(5)[0:n], bcl(small[0:n, 5, :], [n, H, P]), ALU.mult), "on")
                w("oT")
                s(STT(m["OF"][:, 0:4], B4(7)[:, :, 0:n], par[:, 112:113], X[:, 12:16], ALU.mult, ALU.mult), "ofa")
                w("hi")
                s(TT(hlo[:, :, bass.ds(t * P, n)], m["OF"], hhi[:, :, bass.ds(t * P, n)].bitcast(F32),
                     ALU.subtract), "lo")
                if n == NS:
                    gls = keepb[:, 0:2, :].rearrange("p a (b h) -> p (a b) h", h=H)
                    for h in range(H):
                        if h:
                            dve.wait_ge(S("gs_ds"), h)
                        TT(m["VNM"][0:n], bcm(m["VN"][0:n, h], [n, NB, P]), bcl(rowmask[:, :], [n, NB, P]),
                           ALU.mult).then_inc(S("gs_vm"), 1)
                        TT(m["SS"][:, :, h], m["SS"][:, :, h], bcl(gls[:, :, h], [P, NB, P]), ALU.mult)\
                            .then_inc(S("gs_dec"), 1)
                        dve.wait_ge(S("gs_dec"), h + 1)
                        dve.wait_ge(S("gs_ds"), h + 1)
                        for q in range(2):
                            last = TT(m["SS"][:, 4 * q:4 * q + 4, h], m["SS"][:, 4 * q:4 * q + 4, h], B4(q), ALU.add)
                        last.then_inc(S("gs_new"), 1)

            def ml_prep():
                dve.wait_ge(S("gates_sb"), 2)
                dve.wait_ge(S("hvec_loaded"), 64)
                gb = hvec[:, 0:2, :]
                z = gtmp[:, 0, :].rearrange("p (t h) -> p t h", h=H)
                TT(cols[:, :, 0, :], gates[:, :, 0:4], bcm(gb[:, 0], [P, TILES + 1, H]), ALU.add)
                TT(z, gates[:, :, 4:8], bcm(gb[:, 1], [P, TILES + 1, H]), ALU.add).then_inc(S("mz_ready"), 1)
                dve.wait_ge(S("mp"), 3)
                STT(cols[:, :, 1, :], z, 0.0, gtmp[:, 1, :].rearrange("p (t h) -> p t h", h=H), ALU.min,
                    ALU.subtract).then_inc(S("mg_ready"), 1)
                c = [0]

                def link(ins):
                    c[0] += 1
                    ins.then_inc(S("m_row_step"), 1)
                    dve.wait_ge(S("m_row_step"), c[0])

                def tiles(r):
                    return r[0:H, 0:NP].rearrange("p (t n) -> p t n", t=TILES)

                def seqs(r):
                    return r[0:H, NP:T].rearrange("p (b n) -> p b n", b=NB)

                link(dve.memset(RST[0:H, :], 1.0))
                dve.memset(tiles(RST)[:, :, 0:1], 0.0)
                link(dve.memset(seqs(RST)[:, :, 0:1], 0.0))
                dve.wait_ge(S("m_rows_sb"), 2)
                link(dve.tensor_tensor_scan(BR[0:H, :], RST[0:H, :], LF[0:H, :], 0.0, ALU.mult, ALU.add))
                link(dve.tensor_tensor_scan(MR[0:H, 0:NP], LF[0:H, 0:NP], IR[0:H, 0:NP], 0.0, ALU.add, ALU.max))
                dve.memset(D0X[0:H, :, 0:1], -BIG)
                dve.tensor_copy(D1X[0:H, :, 0:1], MPR[0:H, NB:2 * NB].unsqueeze(2))
                dve.tensor_copy(D0X[0:H, :, 1:], seqs(LF))
                link(dve.tensor_copy(D1X[0:H, :, 1:], seqs(IR)))
                flat = lambda r: r[0:H].rearrange("p b s -> p (b s)")
                link(dve.tensor_tensor_scan(flat(MSX), flat(D0X), flat(D1X), 0.0, ALU.add, ALU.max))
                link(dve.tensor_copy(seqs(MR), MSX[0:H, :, 1:]))
                dve.memset(MPR[0:H, 0:1], 0.0)
                dve.tensor_copy(MPR[0:H, 1:TILES].unsqueeze(2), tiles(MR)[:, 0:TILES - 1, P - 1:P])
                for dst, r in ((MLA, MR), (BLA, BR)):
                    dve.tensor_copy(dst[0:H, 0:TILES].unsqueeze(2), tiles(r)[:, :, P - 1:P])
                    last = dve.tensor_copy(dst[0:H, TILES:2 * NB].unsqueeze(2), seqs(r)[:, :, LS - 1:LS])
                link(last)
                TT(AR[0:H, :], IR[0:H, :], BR[0:H, :], ALU.subtract)
                TT(ROWM[0:H, :], BR[0:H, :], MR[0:H, :], ALU.subtract)
                link(TT(BLA[0:H, :], MLA[0:H, :], BLA[0:H, :], ALU.subtract))
                TT(KPR[0:H, :], MPR[0:H, :], BLA[0:H, :], ALU.subtract).then_inc(S("m_keep_in"), 1)
                for v, a, b in ((tiles, 0, TILES), (seqs, NB, 2 * NB)):
                    shape = [H, TILES, P] if v is tiles else [H, NB, LS]
                    TT(v(ROWW), v(ROWM), bcl(MPR[0:H, a:b], shape), ALU.add)
                    last = TT(v(LWR), v(AR), bcl(BLA[0:H, a:b], shape), ALU.subtract)
                link(last)
                dve.sem_inc(S("m_lw_done"), 1)
                dve.memset(CN[:, :, :], 0.0).then_inc(S("g_state"), 1)

            def ml(t, n):
                m = ml_map(n)
                X = m["X"]
                w = lambda name, v=None: dve.wait_ge(S("g_" + name), t + (1 + TILES + 1) if v is None else v)
                s = lambda ins, name: ins.then_inc(S("g_" + name), 1)
                s(dve.tensor_copy(tcol[0:n, 0:3, :].rearrange("p a h -> p (a h)").unsqueeze(1),
                                  cum[0:n, bass.ds(t, 1)]), "tc")
                a, wk, em = (tcol[0:n, i, :] for i in range(3))
                if n == P:
                    s(dve.tensor_copy(small[:, 6, :].unsqueeze(2), keepb[:, :, bass.ds(t, 1)]), "tk")
                w("tc")
                w("bc")
                mn = masknegT if n == P else masknegTS
                for h in range(H):
                    last = STT(m["WTm"][0:n, h], B4(0)[0:n, h, 0:n], a[:, h:h + 1], mn[:, :], ALU.add, ALU.add)
                s(last, "dtu")
                dve.wait_ge(S("g_xin"), (t + (TILES + 2)) * 16)
                w("E")
                s(STT(m["QD"], X[:, 0:4], QSCALE, m["E"], ALU.mult, ALU.mult), "qd" if n == P else "qds")
                if n == NS:
                    w("qds", 2)
                    s(TT(m["QDM"], m["QD"].unsqueeze(2).broadcast_to([P, H, NB, NS]),
                         colmask[:, :, :].unsqueeze(1).broadcast_to([P, H, NB, NS]), ALU.mult), "qd")
                w("kq")
                w("DTe")
                s(STT(m["ST"][0:n], B4(2)[0:n, :, 0:n], QSCALE, m["WTm"][0:n], ALU.mult, ALU.mult), "qk")
                w("kT")
                s(TT(m["KW"][0:n], B4(3)[0:n], bcl(wk, [n, H, P]), ALU.mult), "rhs")
                if n == NS:
                    w("vb")
                    kp = keepb
                    for h in range(H):
                        if h:
                            dve.wait_ge(S("ms_dc"), h * NB)
                        TT(m["VM"][0:n], bcm(m["V1"][0:n, h], [n, NB, DV + 1]), bcl(rowmask[:, :], [n, NB, DV + 1]),
                           ALU.mult).then_inc(S("ms_vm"), 1)
                        for b in range(NB):
                            dve.wait_ge(S("ms_dc"), h * NB + b + 1)
                            cs = m["CS2"][:, h % 2, b, :]
                            STT(cs, cs, kp[:, h, TILES + b:TILES + b + 1], B[2 + b % 4][:, 0:DV + 1],
                                ALU.mult, ALU.add).then_inc(S("ms_upd"), 1)
                w("oss")
                s(TT(small[0:n, 1, :], small[0:n, 1, :], em, ALU.max), "den")
                w("den", t + 1)
                s(dve.reciprocal(small[0:n, 2, :], small[0:n, 1, :]), "rd")
                w("rd", t + 1)
                s(TT(small[0:n, 7, :], small[0:n, 0, :], small[0:n, 2, :], ALU.mult), "ms1")
                w("ms1", t + 1)
                s(TT(small[0:n, 3, :], small[0:n, 7, :], small[0:n, 2, :], ALU.mult), "ms")
                if n == P:
                    w("tk", t + 1)
                    w("ds", t + (TILES + 1))
                    for h in range(H):
                        last = STT(CN[:, h], CN[:, h], small[:, 6, h:h + 1], B[2 + h][:, 0:DV + 1],
                                   ALU.mult, ALU.add)
                    s(last, "state")
                w("ossr")
                s(TT(small[0:n, 7, :], small[0:n, 5, :], small[0:n, 2, :], ALU.mult), "f")
                w("f", t + 1)
                for h in range(H):
                    last = dve.tensor_scalar(m["HN"][0:n, h], B[(0, 1, 6, 7)[h]][0:n, 0:DV], small[0:n, 7, h:h + 1],
                                             None, ALU.mult)
                s(last, "on")
                for q in range(2):
                    w(("z", "oT")[q])
                    s(STT(m["OF"][:, q:8:2], B4(4 + q)[:, :, 0:n], par[:, 117 + q:118 + q], X[:, 16 + q:24:2],
                          ALU.mult, ALU.mult), ("ofa", "ofb")[q])
                w("hi")
                s(TT(hlo[:, :, bass.ds(t * P, n)], m["OF"], hhi[:, :, bass.ds(t * P, n)].bitcast(F32),
                     ALU.subtract), "lo")

            phase = lambda: phase_end(dve, "dve")
            load_x()
            for l in range(2):
                phase()
                pre_norm(4 * l, 2 * l)
                if l == 0:
                    dve.memset(gates[:, :, :], 0.0)
                    dve.memset(cum[:, :, :], 0.0)
                    dve.memset(gtmp[:, :, :], 0.0)
                    dve.memset(cols[:, :, :, :], 0.0).then_inc(S("cols_zero"), 1)
                    dve.sem_inc(S("conv_act"), 2)
                in_proj(l)
                phase()
                if l == 0:
                    gdn_prep()
                    phase()
                    with dve.Fori(0, TILES) as t:
                        dve.wait_ge(S("g_tile"), t * 3 + 3)
                        gdn(t, P, LEVELS, t * LEVELS)
                        dve.drain().then_inc(S("g_tile"), 1)
                    phase()
                    gdn(TILES, NS, LEVELS_S, TILES * LEVELS)
                else:
                    ml_prep()
                    phase()
                    with dve.Fori(0, TILES) as t:
                        dve.wait_ge(S("g_tile"), t * 3 + 3 * (TILES + 1))
                        ml(t, P)
                        dve.drain().then_inc(S("g_tile"), 1)
                    phase()
                    dve.memset(ml_map(NS)["V1"][0:NS, :, DV:DV + 1], 1.0).then_inc(S("ms_ones"), 1)
                    dve.wait_ge(S("ms_ones"), 1)
                    ml(TILES, NS)
                phase()
                with dve.Fori(0, KT // 2) as i:
                    for k in range(2):
                        lo(i * 2 + (U0[l] + U_IN + k + 1), (k + 1) % 2)
                post_norm(4 * l + 1)
                pre_norm(4 * l + 2, 2 * l + 1)
                phase()
                dve.memset(acc[:, :, :], 0.0).then_inc(S("acc_zero"), 1)
                dve.wait_ge(S("acc_zero"), l + 1)
                with dve.Fori(0, FG - 1) as g:
                    ff_group(l, g, False)
                ff_group(l, FG - 1, l == 1)
                phase()
                post_norm(4 * l + 3)
            phase()

        @block.gpsimd
        def _(pool):
            dma = pool.dma_start

            def affine(v, pattern, op, fill, base, mult):
                return pool.affine_select(out=v, in_=v, pattern=pattern, compare_op=op, fill=fill, base=base,
                                          channel_multiplier=mult)

            done = [0]

            def step(ins):
                done[0] += 1
                ins.then_inc(S("const_step"), 1)
                pool.wait_ge(S("const_step"), done[0])

            def constants():
                step(pool.memset(ident[:, :], 0.0))
                step(affine(ident[:, :], [[-1, P]], ALU.not_equal, 1.0, 0, 1))
                pool.sem_inc(S("ident_ready"), 1)
                pool.memset(ones[:, :], 1.0)
                pool.memset(triU[:, :], 1.0)
                pool.memset(maskpos[:, :], 0.0)
                pool.memset(masknegT[:, :], 0.0)
                pool.memset(triUS[:, :], 1.0)
                pool.memset(maskposS[:, :], 0.0)
                pool.memset(masknegTS[:, :], 0.0)
                pool.memset(blk4[:, :], 1.0)
                pool.memset(rowmask[:, :], 1.0)
                pool.memset(colmask[:, :, :], 0.0)
                pool.memset(sel[:, :, :], 0.0)
                step(pool.memset(lmask[:, :, :], 0.0))
                for m, n in ((triU, P), (triUS, NS)):
                    step(affine(m[:, :], [[1, n]], ALU.is_ge, 0.0, 0, -1))
                for m, n in ((maskpos, P), (maskposS, NS)):
                    step(affine(m[:, :], [[-1, n]], ALU.is_gt, BIG, 0, 1))
                for m, n in ((masknegT, P), (masknegTS, NS)):
                    step(affine(m[:, :], [[1, n]], ALU.is_ge, -BIG, 0, -1))
                for m, fill in ((triUS, 0.0), (maskposS, BIG), (masknegTS, -BIG), (blk4, 0.0)):
                    v = m[:, :].rearrange("p (b s) -> p b s", s=LS)
                    step(affine(v, [[-LS, NB], [0, LS]], ALU.is_ge, fill, 0, 1))
                    step(affine(v, [[LS, NB], [0, LS]], ALU.is_ge, fill, LS - 1, -1))
                step(affine(rowmask[:, :], [[-LS, NB]], ALU.is_ge, 0.0, 0, 1))
                step(affine(rowmask[:, :], [[LS, NB]], ALU.is_ge, 0.0, LS - 1, -1))
                for b in range(NB):
                    step(pool.memset(colmask[:, b, b * LS:(b + 1) * LS], 1.0))
                step(affine(sel[:, :, :], [[-1, H], [0, P]], ALU.not_equal, 1.0, 0, 1))
                for q in range(LEVELS):
                    w = 1 << q
                    v = lmask[:, q, :].rearrange("p (b e w) -> p b e w", e=2, w=w)
                    step(pool.memset(v[:, :, 1, :], 1.0))
                    pat = lambda a: [[a, P // (2 * w)], [0, w]]
                    step(affine(v[:, :, 1, :], pat(-2 * w), ALU.is_ge, 0.0, 0, 1))
                    step(affine(v[:, :, 1, :], pat(2 * w), ALU.is_ge, 0.0, w - 1, -1))

            def load_x():
                r = rows_in
                step(pool.memset(r[:, :], 0.0))
                dma(r[0:64, :], norm_g.rearrange("l q (c p) -> (l q c) p", p=P)).then_inc(S("rows_loaded"), 16)
                dma(r[64:112, :], conv_w.rearrange("e j (c p) -> (e j c) p", p=P)).then_inc(S("rows_loaded"), 16)
                dma(r[112:113, :], gdn_norm_g).then_inc(S("rows_loaded"), 16)
                dma(r[113:117, :], sgu_norm_g[0]).then_inc(S("rows_loaded"), 16)
                dma(r[117:119, :], mlstm_norm_g.rearrange("e (c p) -> (e c) p", p=P)).then_inc(S("rows_loaded"), 16)
                dma(r[119:123, :], sgu_b[0]).then_inc(S("rows_loaded"), 16)
                for t in range(2):
                    dma(x_tm[:, t, :], x_prompt[0, t * P:(t + 1) * P, :]).then_inc(S(f"x_loaded{t}"), 16)

            def load_x_rest():
                with pool.Fori(0, TILES // 2 - 1) as i:
                    for k in range(2):
                        pool.wait_ge(S("x_turned"), i * 4 + (2 * k + 2))
                        dma(x_tm[:, k, :], x_prompt[0, bass.ds(i * (2 * P) + (k + 2) * P, P), :])\
                            .then_inc(S(f"x_loaded{k}"), 16)
                pool.wait_ge(S("x_turned"), 2 * TILES - 2)
                dma(x_tm[0:NS, 0, :], x_sample.rearrange("b s d -> (b s) d")).then_inc(S("x_loaded0"), 16)

            def residual(p):
                for c in range(KT):
                    pool.wait_ge(S("mix_normed"), KT * p + c + 1)
                    pool.tensor_tensor(xT[:, c], xT[:, c], hf2[:, c % 2], ALU.add).then_inc(S("x_ready"), 1)

            def in_proj(l):
                pr = proj[l]
                if l == 0:
                    dma(cs_tm[0:24, :], state_gdn_conv[0].rearrange("b j c -> (b j) c")).then_inc(S("wg_loaded"), 16)
                dma(wg[:, :, :], w_in[l][0, :, GATE0:GATE0 + 2 * H].rearrange("(t p) n -> p t n", p=P))\
                    .then_inc(S("wg_loaded"), 16)

                def send(i, c0, k):
                    dst = pr[bass.ds(i * 2 + (c0 + k), 1)].rearrange("a p t -> (a p) t")
                    dma(dst, pout2[:, k]).then_inc(S("stored"), 16)
                    pool.wait_ge(S("stored"), i * 32 + 16 * (l * NCH + c0 + k + 1))
                    pool.sem_inc(S("row_free"), 1)

                if l == 0:
                    with pool.Fori(0, NCONV // 2) as i:
                        for k in range(2):
                            pool.wait_ge(S("conv_act"), i * 2 + (2 + k + 1))
                            send(i, 0, k)
                    first = NCONV
                else:
                    first = 0
                with pool.Fori(0, (NCH - first) // 2) as i:
                    for k in range(2):
                        pool.wait_ge(S("act_evac"), i * 6 + (AE0[l] + BANKS + (first + k + 1) * TG))
                        send(i, first, k)
                if l == 0:
                    pool.wait_ge(S("tails_sb"), 1)
                    dma(conv_p[0, 0], tail_tm[0:3, :]).then_inc(S("state_out"), 16)
                    dma(conv_s[0].rearrange("b j c -> (b j) c"), tail_tm[3:27, :]).then_inc(S("state_out"), 16)
                    pool.wait_ge(S("state_out"), 32)

            def gdn_prep():
                dma(hvec[:, 0, :], a_log.broadcast_to([P, H])).then_inc(S("hvec_loaded"), 16)
                dma(hvec[:, 1, :], dt_bias.broadcast_to([P, H])).then_inc(S("hvec_loaded"), 16)
                dma(sgw_in, sgu_w[0].rearrange("g p q -> p g q")).then_inc(S("sgw_loaded"), 16)
                step(pool.memset(WTS[0:NS], 0.0))
                for b in range(NB):
                    dma(WTS[b * LS:(b + 1) * LS, :, b * LS:(b + 1) * LS],
                        sgu_w[0, :, 0:LS, 0:LS].rearrange("g p q -> p g q")).then_inc(S("sgw_loaded"), 16)
                dma(BROW[0:1], sgu_b[0:1]).then_inc(S("sgw_loaded"), 16)
                dma(GSG, sgu_norm_g.broadcast_to([P, H, P])).then_inc(S("sgw_loaded"), 16)
                dma(BROWS[0:1, :, 0:1, :], sgu_b[0:1, :, 0:LS].unsqueeze(2))\
                    .then_inc(S("sgw_loaded"), 16)
                pool.wait_ge(S("sgw_loaded"), 16 * (4 + NB))
                step(pool.tensor_copy(BROWS[0:1, :, 1:, :], BROWS[0:1, :, 0:1, :].broadcast_to([1, H, NB - 1, LS])))

            def tile_in(l, t, n, X, name):
                src = proj[l][:, :, bass.ds(t * P, n)].rearrange("c p t -> p c t")
                dma(X, src).then_inc(S(name), 16)

            def out_state(m, h):
                cs = m["CS2"][:, h % 2]
                pool.wait_ge(S("ms_upd"), (h + 1) * NB)
                dma(c_s[0, :, h].rearrange("b k v -> k b v"), cs[:, :, 0:DV]).then_inc(S(f"cs_out{h % 2}"), 16)
                with nc.allow_non_contiguous_dma("1024 numbers"):
                    dma(n_s[0, :, h].rearrange("b k -> k b").unsqueeze(2), cs[:, :, DV:DV + 1])\
                        .then_inc(S(f"cs_out{h % 2}"), 16)

            constants()
            load_x()
            pool.sem_inc(S("w_used"), 2)
            pool.sem_inc(S("row_free"), 2)
            load_x_rest()
            phase = lambda: phase_end(pool, "pool")
            for l in range(2):
                phase()
                in_proj(l)
                phase()
                if l == 0:
                    gdn_prep()
                    phase()
                    pool.sem_inc(S("g_tile"), 3)
                    with pool.Fori(0, TILES) as t:
                        pool.wait_ge(S("g_tile"), t * 3 + 3)
                        tile_in(0, t, P, gdn_map(P)["X"], "g_xin")
                    pool.wait_ge(S("g_state"), TILES + 1)
                    dma(gdn_p[0, 0].rearrange("h k v -> k h v"), St[:, :, :]).then_inc(S("state_out"), 16)
                    phase()
                    m = gdn_map(NS)
                    dma(m["SS"], state_gdn[0].rearrange("b h k v -> k b h v")).then_inc(S("wg_loaded"), 16)
                    pool.wait_ge(S("wg_loaded"), 16 * 3)
                    tile_in(0, TILES, NS, m["X"], "g_xin")
                    pool.wait_ge(S("g_vb"), TILES + 1)
                    dma(sguv_s[0].rearrange("b s c -> (b s) c"), m["VB"][0:NS].rearrange("p g c -> p (g c)"))\
                        .then_inc(S("state_out"), 16)
                    pool.wait_ge(S("gs_new"), H)
                    dma(gdn_s[0].rearrange("b h k v -> k b h v"), m["SS"]).then_inc(S("state_out"), 16)
                    pool.wait_ge(S("state_out"), 16 * 5)
                else:
                    dma(hvec[:, 0:2, :], gate_b_odd.rearrange("e (a h) -> e a h", a=2).broadcast_to([P, 2, H]))\
                        .then_inc(S("hvec_loaded"), 16)
                    with nc.allow_non_contiguous_dma("32 numbers"):
                        dma(MPR[0:H, NB:2 * NB].unsqueeze(2), state_mlstm_m[0].rearrange("b h -> h b").unsqueeze(2))\
                            .then_inc(S("hvec_loaded"), 16)
                    pool.wait_ge(S("m_row_step"), 10)
                    with nc.allow_non_contiguous_dma("36 numbers"):
                        dma(m_p[0, 0:1].rearrange("b h -> h b"), MLA[0:H, TILES - 1:TILES]).then_inc(S("state_out"), 16)
                        dma(m_s[0].rearrange("b h -> h b").unsqueeze(2), MLA[0:H, TILES:2 * NB].unsqueeze(2))\
                            .then_inc(S("state_out"), 16)
                    pool.wait_ge(S("state_out"), 16 * 7)
                    phase()
                    step(pool.memset(ml_map(P)["V1"][:, :, DV:DV + 1], 1.0))
                    with pool.Fori(0, TILES) as t:
                        pool.wait_ge(S("g_tile"), t * 3 + 3 * (TILES + 1))
                        tile_in(1, t, P, ml_map(P)["X"], "g_xin")
                    pool.wait_ge(S("g_state"), 2 * TILES + 2)
                    dma(c_p[0, 0].rearrange("h k v -> k h v"), CN[:, :, 0:DV]).then_inc(S("state_out"), 16)
                    with nc.allow_non_contiguous_dma("512 numbers"):
                        dma(n_p[0, 0].rearrange("h k -> k h").unsqueeze(2), CN[:, :, DV:DV + 1])\
                            .then_inc(S("state_out"), 16)
                    phase()
                    m = ml_map(NS)
                    tile_in(1, TILES, NS, m["X"], "g_xin")
                    for h in range(H):
                        cs = m["CS2"][:, h % 2]
                        if h >= 2:
                            pool.wait_ge(S(f"cs_out{h % 2}"), 32 * (h // 2))
                        dma(cs[:, :, 0:DV], state_mlstm_c[0, :, h].rearrange("b k v -> k b v"))\
                            .then_inc(S(f"ms_cin{h % 2}"), 16)
                        with nc.allow_non_contiguous_dma("1024 numbers"):
                            dma(cs[:, :, DV:DV + 1], state_mlstm_n[0, :, h].rearrange("b k -> k b").unsqueeze(2))\
                                .then_inc(S(f"ms_cin{h % 2}"), 16)
                        if h >= 1:
                            out_state(m, h - 1)
                    out_state(m, H - 1)
                    pool.wait_ge(S("state_out"), 16 * 9)
                    for k in range(2):
                        pool.wait_ge(S(f"cs_out{k}"), 64)
                phase()
                residual(2 * l)
                phase()
                phase()
                residual(2 * l + 1)
            phase()
            for t in range(TILES + 1):
                pool.wait_ge(S("y_copied"), 2 * t + 2)
                n = P if t < TILES else NS
                dst = y_prompt[0, t * P:(t + 1) * P, :] if t < TILES else y_sample.rearrange("b s d -> (b s) d")
                dma(dst, x_tm[0:n, t % 2, :]).then_inc(S(f"y_stored{t % 2}"), 16)
            pool.wait_ge(S("y_stored0"), 16 * 5)
            pool.wait_ge(S("y_stored1"), 16 * 4)


_INS = ['x_prompt', 'x_sample', 'state_gdn', 'state_gdn_conv', 'state_mlstm_c', 'state_mlstm_n', 'state_mlstm_m',
        'norm_g', 'w_in_even', 'conv_w', 'a_log', 'dt_bias', 'gdn_norm_g', 'sgu_norm_g', 'sgu_w', 'sgu_b',
        'w_out_even', 'w_in_odd', 'gate_b_odd', 'mlstm_norm_g', 'w_out_odd', 'w_ff1', 'w_ff2']
_OUTS = [(1, 1024, 1024), (8, 4, 1024), (1, 1, 4, 128, 128), (1, 8, 4, 128, 128), (1, 1, 3, 1536), (1, 8, 3, 1536),
         (1, 8, 4, 512), (1, 1, 4, 128, 256), (1, 8, 4, 128, 256), (1, 1, 4, 128), (1, 8, 4, 128), (1, 1, 4),
         (1, 8, 4)]


def kernel(**inputs):
    import numpy as _np
    import concourse.bacc as _bacc
    from concourse import mybir as _mybir
    from concourse.bass_utils import run_bass_kernel_spmd as _run

    nc = _bacc.Bacc("TRN2", target_bir_lowering=False, num_devices=1)
    arrays, args = {}, []
    for name in _INS:
        a = _np.ascontiguousarray(inputs[name])
        arrays[f"in_{name}_dram"] = a
        args.append(nc.dram_tensor(f"in_{name}_dram", a.shape, _mybir.dt.from_np(a.dtype), kind="ExternalInput").ap())
    for i, shape in enumerate(_OUTS):
        args.append(nc.dram_tensor(f"out_{i}_dram", shape, _mybir.dt.float32, kind="ExternalOutput").ap())
    build(nc, *args)
    r = _run(nc, [arrays], core_ids=[0])
    return tuple(r.results[0][f"out_{i}_dram"] for i in range(len(_OUTS)))
```

```python
from contextlib import ExitStack

import concourse.bass as bass
from concourse import mybir

F32 = mybir.dt.float32
F32R = mybir.dt.float32r
ALU = mybir.AluOpType
ACT = mybir.ActivationFunctionType

P = 128
D = 1024
KT = D // P
NP = 1024
NB, LS = 8, 4
NS = NB * LS
T = NP + NS
TG = 3
N = T // TG
TILES = NP // P
H = 4
DFF = 4 * D
CONVW = 4
NCONV = 12
NCH = 24
GATE0 = 2048
DV = 256
EPS = 1e-6
BIG = 1e30
QSCALE = P ** -0.5
LEVELS = 7
LEVELS_S = 2
XC = 3 + NP
XCW = XC + NB * (3 + LS)
FG = 8
FK = DFF // P // FG

U_IN, U_OUT, U_FF = NCH, KT, FG * 2 * FK
U_LAYER = U_IN + U_OUT + U_FF
J_IN, J_OUT, J_W1, J_W2 = TG * NCH, TG * KT, TG * FK, TG * KT
J_LAYER = J_IN + J_OUT + FG * (J_W1 + J_W2)
A_LAYER = J_IN + J_OUT + FG * J_W1
D_LAYER = FG * J_W2
RS = 384
BANKS = 6


def build(nc, x_prompt, x_sample, state_gdn, state_gdn_conv, state_mlstm_c, state_mlstm_n, state_mlstm_m,
          norm_g, w_in_even, conv_w, a_log, dt_bias, gdn_norm_g, sgu_norm_g, sgu_w, sgu_b, w_out_even,
          w_in_odd, gate_b_odd, mlstm_norm_g, w_out_odd, w_ff1, w_ff2,
          y_prompt, y_sample, gdn_p, gdn_s, conv_p, conv_s, sguv_s, c_p, c_s, n_p, n_s, m_p, m_s):
    ctx = ExitStack()
    with ctx:
        sems = {}

        def S(name):
            if name not in sems:
                sems[name] = ctx.enter_context(nc.semaphore(name))
            return sems[name]

        def sb(name, shape, dt=F32):
            return ctx.enter_context(nc.sbuf_tensor(name, shape, dt))

        xT = sb("xT", [P, KT, T])
        hhi = sb("hhi", [P, KT, T], F32R)
        hlo = sb("hlo", [P, KT, T], F32R)
        wst = sb("wst", [P, 2, 1024])
        whi = sb("whi", [P, 2, 1024], F32R)
        wlo = sb("wlo", [P, 2, 1024], F32R)
        arena_at = -(-nc.sbuf_base // 32) * 32
        arena = sb("arena", [P, 2 * KT * T])

        ident = sb("ident", [P, P])
        ones = sb("ones", [P, P])
        maskpos = sb("maskpos", [P, P])
        masknegT = sb("masknegT", [P, P])
        maskposS = sb("maskposS", [NS, NS])
        masknegTS = sb("masknegTS", [NS, NS])
        triU = sb("triU", [P, P])
        triUS = sb("triUS", [NS, NS])
        blk4 = sb("blk4", [NS, NS])
        lmask = sb("lmask", [P, LEVELS, P])
        rowmask = sb("rowmask", [NS, NB])
        colmask = sb("colmask", [P, NB, NS])
        sel = sb("sel", [H, H, P])
        par = sb("par", [P, P])
        gates = sb("gates", [P, TILES + 1, 2 * H])
        wg = sb("wg", [P, KT, 2 * H])
        wg_hi = sb("wg_hi", [P, KT, 2 * H], F32R)
        wg_lo = sb("wg_lo", [P, KT, 2 * H], F32R)
        cols = sb("cols", [P, TILES + 1, 6, H])
        tcol = sb("tcol", [P, 6, H])
        small = sb("small", [P, 8, H])
        gtmp = sb("gtmp", [P, 4, (TILES + 1) * H])
        hvec = sb("hvec", [P, 4, H])
        keepb = sb("keepb", [P, H, 2 * NB])
        epsc = sb("epsc", [P, 1])
        rows4 = sb("rows4", [H, 2, P])

        def psum(name):
            return ctx.enter_context(nc.psum_tensor(name, [P, 512], F32))

        B = [psum(f"bank{i}") for i in range(8)]

        def B4(i):
            return B[i][:, :].rearrange("p (h n) -> p h n", h=4)


        def carve(*shapes, at=0):
            out = []
            for shape in shapes:
                size = 1
                for s in shape:
                    size *= s
                v = arena[:, at:at + size]
                if len(shape) > 1:
                    names = "abcd"[:len(shape)]
                    v = v.rearrange("p (" + " ".join(names) + ") -> p " + " ".join(names),
                                    **dict(zip(names, shape)))
                out.append(v)
                at += size
            assert at <= 2 * KT * T, at
            return out

        acc, sq2, ssum, lnss, rstd, hf2 = carve((KT, T), (2, T), (T,), (T,), (T,), (2, T))
        half = arena_at + 4 * KT * T
        h1hi = nc.alloc_sbuf_tensor_at("h1hi", [P, FK, T], F32R, offset=half)
        h1lo = nc.alloc_sbuf_tensor_at("h1lo", [P, FK, T], F32R, offset=half + 4 * FK * T)
        x_tm, rows_in = carve((2, D), (P,))
        xc2, cy2, pout2, cs_tm = carve((2, XCW), (2, T), (2, T), (NCONV * P,))
        tail_tm = carve((NCONV * P,), at=KT * T)[0]
        gT = carve((T,), at=(KT + 3) * T)[0]
        csT, tails, cw2 = carve((NCONV, NB * 3), (NCONV, 3 + NB * 3), (2, CONVW), at=(KT + 7) * T)
        St, GR, WT, WTS, BROW, BROWS, GSG = carve(
            (H, P), (T,), (H, P), (H, NS), (H, P), (H, NB, LS), (H, P))
        gdn_at = 4 * H * P + T + 2 * H * NS
        sgw_in = carve((H, P), at=7000)[0]
        CN, ROWM, ROWW = carve((H, DV + 1), (T,), (T,))
        ml_at = H * (DV + 1) + 2 * T + 4
        IR, LF, BR, MR, AR, LWR, RST, MSX, D0X, D1X, MPR, MLA, BLA, KPR = carve(
            (T,), (T,), (T,), (T,), (T,), (T,), (T,), (NB, LS + 1), (NB, LS + 1), (NB, LS + 1),
            (2 * NB,), (2 * NB,), (2 * NB,), (2 * NB,), at=ml_at)
        relu2 = sb("relu2", [P, 2, N])
        cum = sb("cum", [P, TILES + 1, 12])

        def gdn_map(n):
            keys = ["X", "QH", "SQ", "RB", "OF", "DT", "A", "QD", "NW", "XX", "RW", "KD", "RU", "VN", "ON", "VB"]
            shapes = [(NCH, n), (8, n), (8, n), (8, n), (8, n)] + [(H, n)] * 4 + [(2, 2 * 2, n)] + [(H, P)] * 6
            if n == NS:
                keys += ["SS", "NWM", "QDM", "VNM"]
                shapes += [(NB, H, P), (H, NB, NS), (H, NB, NS), (NB, P)]
            m = dict(zip(keys, carve(*shapes, at=gdn_at)))
            m["Dm"], m["E"] = m["SQ"][:, 0:4], m["SQ"][:, 4:8]
            m["T2"] = m["RB"][:, 0:4]
            m["Xi"] = lambda h: m["XX"][0:n, h // 2, h % 2, :]
            m["XiT"] = lambda h: m["XX"][0:n, h // 2, 2 + h % 2, :]
            return m

        def ml_map(n, k=0):
            keys = ["X2", "WTm", "E", "QD", "ST", "OF", "KW", "V1", "HN"]
            shapes = [(2, NCH, n), (H, n), (H, n), (H, n), (H, n), (8, n), (H, P), (H, DV + 1), (H, DV)]
            if n == NS:
                keys += ["CS2", "QDM", "VM"]
                shapes += [(2, NB, DV + 1), (H, NB, NS), (NB, DV + 1)]
            m = dict(zip(keys, carve(*shapes, at=ml_at)))
            m["X"] = m["X2"][:, k]
            return m

        proj = [nc.dram_tensor(f"proj{l}", (NCH, P, T), F32) for l in range(2)]

        def accd(c, tg):
            return acc[:, bass.ds(c, 1), tg * N:(tg + 1) * N]

        phases = {}

        def phase_end(eng, who, wait=True):
            phases[who] = phases.get(who, 0) + 1
            eng.drain().then_inc(S("phase_end"), 1)
            if wait:
                eng.wait_ge(S("phase_end"), 4 * phases[who])

        w_in = [w_in_even, w_in_odd]
        w_out = [w_out_even, w_out_odd]
        U0 = [0, U_LAYER]
        J0 = [0, J_LAYER]
        AE0 = [0, A_LAYER]
        DE0 = [0, D_LAYER]

        def in_cols(c):
            return c * P + (2 * H if c >= GATE0 // P else 0)

        block = ctx.enter_context(nc.Block())

        @block.sync
        def _(sp):
            def load(u, k, src):
                sp.wait_ge(S("w_split"), u + 1)
                dst = wst[:, k % 2, :]
                if len(src.shape) == 3:
                    dst = dst.rearrange("p (a b) -> p a b", a=src.shape[1])
                sp.dma_start(dst, src).then_inc(S(f"w_loaded{k % 2}"), 16)

            def cols_of(w, c0):
                return w[:, bass.ds(c0, P)].rearrange("(t p) n -> p t n", p=P)

            for t in range(2):
                sp.dma_start(x_tm[:, t, :], x_prompt[0, t * P:(t + 1) * P, :]).then_inc(S(f"x_loaded{t}"), 16)
            with sp.Fori(0, TILES // 2 - 1) as i:
                for k in range(2):
                    sp.wait_ge(S("x_turned"), i * 4 + (2 * k + 2))
                    sp.dma_start(x_tm[:, k, :], x_prompt[0, bass.ds(i * (2 * P) + (k + 2) * P, P), :])\
                        .then_inc(S(f"x_loaded{k}"), 16)
            sp.wait_ge(S("x_turned"), 2 * TILES - 2)
            sp.dma_start(x_tm[0:NS, 0, :], x_sample.rearrange("b s d -> (b s) d")).then_inc(S("x_loaded0"), 16)
            for l in range(2):
                u = U0[l]
                with sp.Fori(0, 8) as i:
                    for k in range(2):
                        load(i * 2 + (u + k), k, cols_of(w_in[l][0], i * (2 * P) + k * P))
                if l == 0:
                    sp.wait_ge(S("conv_act"), 2 + NCONV)
                    sp.wait_ge(S("tails_ready"), 2 + NCONV)
                    sp.wait_ge(S("filled"), 1)
                    one = lambda dst, src: sp.dma_start(dst, src).then_inc(S("sgw_loaded"), 16)
                    one(sgw_in, sgu_w[0].rearrange("g p q -> p g q"))
                    for b in range(NB):
                        one(WTS[b * LS:(b + 1) * LS, :, b * LS:(b + 1) * LS],
                            sgu_w[0, :, 0:LS, 0:LS].rearrange("g p q -> p g q"))
                    one(BROW[0:1], sgu_b[0:1])
                    one(GSG, sgu_norm_g.broadcast_to([P, H, P]))
                    one(BROWS[0:1, :, 0:1, :], sgu_b[0:1, :, 0:LS].unsqueeze(2))
                with sp.Fori(0, 4) as i:
                    for k in range(2):
                        load(i * 2 + (u + 16 + k), k, cols_of(w_in[l][0], i * (2 * P) + (in_cols(16) + k * P)))
                with sp.Fori(0, 4) as i:
                    for k in range(2):
                        load(i * 2 + (u + U_IN + k), k, cols_of(w_out[l][0], i * (2 * P) + k * P))
                with sp.Fori(0, FG) as g:
                    ug = u + U_IN + U_OUT
                    for k in range(FK):
                        load(g * (2 * FK) + (ug + k), k, cols_of(w_ff1[l], g * (FK * P) + k * P))
                    for k in range(FK):
                        rows = w_ff2[l][bass.ds(g * (FK * P), FK * P), 2 * k * P:2 * (k + 1) * P]
                        load(g * (2 * FK) + (ug + FK + k), k, rows.rearrange("(t p) n -> p t n", p=P))

        @block.tensor
        def _(pe):
            def mm(out, lhsT, rhs, start=True, stop=True):
                return pe.matmul(out, lhsT, rhs, start=start, stop=stop)

            def job(kt, bank, w, xhi, xlo, tg):
                n = 0
                for (a, b) in ((whi, xhi), (whi, xlo), (wlo, xhi)):
                    for t in range(kt):
                        last = mm(B[bank][:, 0:N], w(a, t), b[:, t, tg * N:(tg + 1) * N],
                                  start=n == 0, stop=n == 3 * kt - 1)
                        n += 1
                return last

            def w_ready(u):
                pe.wait_ge(S("w_split"), u + 3)

            def unit8(u, k, wait_bank, split0=None):
                w_ready(u)
                if split0 is None:
                    for tg in range(TG):
                        wait_bank(k * TG + tg)
                        last = job(KT, (k % 2) * TG + tg, lambda a, t: a[:, k % 2, t * P:(t + 1) * P], hhi, hlo, tg)
                        last.then_inc(S("job_done"), 1)
                    pe.drain().then_inc(S("w_used"), 1)
                    return
                for tg in range(TG):
                    wait_bank(k * TG + tg)
                for t in range(KT):
                    pe.wait_ge(S("h_split"), split0 + t + 1)
                    for tg in range(TG):
                        bank = B[(k % 2) * TG + tg][:, 0:N]
                        tok = slice(tg * N, (tg + 1) * N)
                        mm(bank, whi[:, k % 2, t * P:(t + 1) * P], hhi[:, t, tok], start=t == 0, stop=False)
                        mm(bank, whi[:, k % 2, t * P:(t + 1) * P], hlo[:, t, tok], start=False, stop=False)
                    for tg in range(TG):
                        last = mm(B[(k % 2) * TG + tg][:, 0:N], wlo[:, k % 2, t * P:(t + 1) * P],
                                  hhi[:, t, tg * N:(tg + 1) * N], start=False, stop=t == KT - 1)
                        if t == KT - 1:
                            last.then_inc(S("job_done"), 1)
                pe.drain().then_inc(S("w_used"), 1)

            def linear(u0, a0, iters, split0=None):
                with pe.Fori(0, iters) as i:
                    for k in range(2):
                        unit8(i * 2 + (u0 + k), k,
                              lambda j: pe.wait_ge(S("act_evac"), i * BANKS + (a0 + j + 1)),
                              split0 if k == 0 else None)

            def load_x():
                pe.wait_ge(S("ident_ready"), 1)
                pe.wait_ge(S("rows_loaded"), 16 * 6)
                pe.transpose(B[6][:, 0:P], rows_in[:, 0:P], ident[:, :]).then_inc(S("par_T"), 1)
                with pe.Fori(0, TILES // 2) as i:
                    for k in range(2):
                        pe.wait_ge(S(f"x_loaded{k}"), i * 16 + 16)
                        for q in range(2):
                            pe.wait_ge(S("xT_copied"), i * 4 + (2 * k + q + 1))
                            for c in range(4):
                                last = pe.transpose(B[2 * k + q][:, c * P:(c + 1) * P],
                                                    x_tm[:, k, (4 * q + c) * P:(4 * q + c + 1) * P], ident[:, :])
                            last.then_inc(S("x_turned"), 1)
                pe.wait_ge(S("x_loaded0"), 16 * (TILES // 2 + 1))
                for q in range(2):
                    pe.wait_ge(S("xT_copied"), 2 * TILES + q + 1)
                    for c in range(4):
                        last = pe.transpose(B[q][:, c * NS:(c + 1) * NS],
                                            x_tm[0:NS, 0, (4 * q + c) * P:(4 * q + c + 1) * P], ident[0:NS, 0:NS])
                    last.then_inc(S("x_turned"), 1)

            def norm(nn):
                pe.wait_ge(S("squares_added"), KT * (nn + 1))
                for tg in range(TG):
                    last = mm(B[tg][:, 0:N], ones[:, :], ssum[:, tg * N:(tg + 1) * N])
                last.then_inc(S("sumsq"), 1)

            def gate_cols(l):
                pe.wait_ge(S("wg_split"), l + 1)
                pe.wait_ge(S("act_evac"), BANKS + AE0[l] + J_IN)
                for tg in range(TG):
                    k = 0
                    for a, x in ((wg_hi, hhi), (wg_hi, hlo), (wg_lo, hhi)):
                        for c in range(KT):
                            last = mm(B[(6, 7, 3)[tg]][0:2 * H, 0:N], a[:, c, :], x[:, c, tg * N:(tg + 1) * N],
                                      start=k == 0, stop=k == 3 * KT - 1)
                            k += 1
                last.then_inc(S("gate_rows"), 1)

            def gate_turn(l):
                pe.wait_ge(S("gate_rows_sb"), l + 1)
                for t in range(TILES + 1):
                    n = P if t < TILES else NS
                    last = pe.transpose(B[4][0:n, t * 8:t * 8 + 8], gT[0:2 * H, t * P:t * P + n],
                                        ident[0:2 * H, 0:2 * H])
                last.then_inc(S("gates_done"), 1)

            def ff(l):
                u0 = U0[l] + U_IN + U_OUT
                a0 = AE0[l] + J_IN + J_OUT
                d0 = DE0[l]
                with pe.Fori(0, FG) as g:
                    def bank1(j):
                        if j < BANKS:
                            pe.wait_ge(S("dve_evac"), g * J_W2 + (d0 + j + 1))
                        else:
                            pe.wait_ge(S("act_evac"), g * J_W1 + (a0 + j + 1))
                    for k in range(FK):
                        unit8(g * (2 * FK) + (u0 + k), k, bank1, KT * (2 * l + 1) if k == 0 else None)
                    for k in range(FK):
                        w_ready(g * (2 * FK) + (u0 + FK + k))
                        for oc in range(2):
                            for tg in range(TG):
                                j = (2 * k + oc) * TG + tg
                                if j < TG:
                                    pe.wait_ge(S("h1_split"), g * J_W1 + (l * FG * J_W1 + (FK - 1) * TG + tg + 3))
                                if j >= BANKS:
                                    pe.wait_ge(S("dve_evac"), g * J_W2 + (d0 + j + 1))
                                job(FK, j % BANKS,
                                    lambda a, t: a[:, k % 2, t * 2 * P + oc * P:t * 2 * P + (oc + 1) * P],
                                    h1hi, h1lo, tg).then_inc(S("job_done"), 1)
                        pe.drain().then_inc(S("w_used"), 1)

            def conv_tails():
                pe.wait_ge(S("tails_ready"), 2 + NCONV)
                pe.wait_ge(S("act_evac"), BANKS + J_IN)
                for c in range(NCONV):
                    last = pe.transpose(B[c // 4][0:27, (c % 4) * P:(c % 4 + 1) * P], tails[:, c, :], ident[:, :])
                last.then_inc(S("tails_T"), 1)

            def gdn_prep():
                pe.wait_ge(S("cols_g"), 1)
                mm(B[7][:, 0:32], triU[:, :], cols[:, 0:TILES, 5, :])
                mm(B[7][0:NS, 32:36], triUS[:, :], cols[0:NS, TILES, 5, :])
                mm(B[7][:, 36:68], ones[:, :], cols[:, 0:TILES, 5, :])
                mm(B[7][0:NS, 68:72], blk4[:, :], cols[0:NS, TILES, 5, :])
                pe.wait_ge(S("cols_g"), 2)
                mm(B[7][:, 72:104], ones[0:NS, :], gtmp[0:NS, 3, 0:32]).then_inc(S("cum_done"), 1)
                pe.wait_ge(S("gc_ready"), 1)
                for t in range(TILES + 1):
                    n = P if t < TILES else NS
                    last = pe.transpose(B[t // 4][0:H, (t % 4) * P:(t % 4) * P + n], cols[0:n, t, 0, :],
                                        ident[0:n, 0:n])
                last.then_inc(S("gc_rows"), 1)
                pe.wait_ge(S("sgw_loaded"), 16 * (4 + NB))
                for g in range(H):
                    pe.transpose(B4(3)[:, g, :], sgw_in[:, g, :], ident[:, :])
                    last = pe.transpose(B[4][0:NS, g * NS:(g + 1) * NS], WTS[0:NS, g, :], ident[0:NS, 0:NS])
                last.then_inc(S("sgw_T"), 1)

            def gdn_sums(t, n):
                m = gdn_map(n)
                pe.wait_ge(S("g_sq"), t + 1)
                mm(B4(0)[:, :, 0:n], ones[:, :], m["SQ"][:, 0:4, :])
                mm(B4(1)[:, :, 0:n], ones[:, :], m["SQ"][:, 4:8, :]).then_inc(S("g_ss"), 1)

            def gdn_decays(t, n):
                pe.wait_ge(S("g_gr"), t + 1)
                for h in range(H):
                    last = mm(B4(2)[:, h, 0:n], sel[:, h, :], rows4[:, 0, 0:n])
                last.then_inc(S("g_bc"), 1)

            def gdn_v(t, n):
                for g in range(H):
                    last = pe.transpose(B4(7)[0:n, g, :], gdn_map(n)["X"][:, 20 + g, :], ident[:, :])
                last.then_inc(S("g_vsT"), 1)

            def gdn_kk(t, n):
                QH = gdn_map(n)["QH"]
                pe.wait_ge(S("g_kn"), t + 1)
                for h in range(H):
                    last = mm(B4(3)[0:n, h, 0:n], QH[:, 4 + h, :], QH[:, 4 + h, :])
                last.then_inc(S("g_kk"), 1)

            def gdn(t, n, lv, lv0, more=False):
                m = gdn_map(n)
                X, QH, SQ, OF = m["X"], m["QH"], m["SQ"], m["OF"]
                w = lambda name, v=None: pe.wait_ge(S("g_" + name), t + 1 if v is None else v)
                s = lambda ins, name: ins.then_inc(S("g_" + name), 1)
                for h in range(H):
                    last = pe.transpose(B4(6)[0:n, h, :], X[:, 8 + h, :], ident[:, :])
                s(last, "vT")
                w("qn")
                for h in range(H):
                    last = mm(B4(4)[0:n, h, 0:n], QH[:, 4 + h, :], QH[:, h, :])
                s(last, "kq")
                for h in range(H):
                    last = pe.transpose(B4(5)[0:n, h, :], QH[:, 4 + h, :], ident[:, :])
                s(last, "kT")

                def gating():
                    w("vb")
                    wt, br = (WT, BROW) if n == P else (WTS, BROWS.rearrange("p g b l -> p g (b l)"))
                    for g in range(H):
                        mm(B4(3)[:, g, 0:n], m["VB"][0:n, g, :], wt[0:n, g, 0:n], start=True, stop=False)
                        last = mm(B4(3)[:, g, 0:n], ones[0:1, :], br[0:1, g, 0:n], start=False, stop=True)
                    s(last, "z")

                w("A")
                w("Xinit")
                w("vsr")
                w("qk")
                for q in range(lv):
                    for p in range(2):
                        if q:
                            w("inv", lv0(2 * q - 1 + p))
                        for h in (2 * p, 2 * p + 1):
                            last = mm(B4((0, 7)[p])[0:n, h % 2, 0:n], m["A"][0:n, h, :], m["XiT"](h))
                        s(last, "t2")
                    if q == 2:
                        gating()
                    for p in range(2):
                        w("t2s", lv0(2 * q + 1 + p))
                        for h in (2 * p, 2 * p + 1):
                            if q < lv - 1:
                                mm(B4(1 + p)[0:n, h % 2, 0:n], m["T2"][0:n, h, :], m["Xi"](h))
                            last = mm(B4(1 + p)[0:n, 2 + h % 2, 0:n], m["Xi"](h), m["T2"][0:n, h, :])
                        s(last, "x")
                w("inv", lv0(2 * lv))
                if lv <= 2:
                    gating()
                w("rhs")
                w("ofb")
                for h in range(H):
                    last = mm(B4(3)[:, h, 0:n], m["RW"][0:n, h, :], m["XiT"](h))
                s(last, "w")
                if more:
                    gdn_sums(t + 1, n)
                w("state")
                w("nw")
                if n == NS:
                    pe.wait_ge(S("wg_loaded"), 16 * 3)
                for h in range(H):
                    mm(B4(4)[0:n, h, :], m["XiT"](h), m["RU"][0:n, h, :], start=True, stop=False)
                    if n == P:
                        last = mm(B4(4)[0:n, h, :], m["NW"][:, h, :], St[:, h, :], start=False, stop=True)
                    else:
                        for b in range(NB):
                            last = mm(B4(4)[0:n, h, :], m["NWM"][:, h, b, :], m["SS"][:, b, h, :],
                                      start=False, stop=b == NB - 1)
                s(last, "vnew")
                if more:
                    gdn_decays(t + 1, n)
                w("vns")
                w("qd")
                for h in range(H):
                    if n == P:
                        mm(B4(5)[0:n, h, :], m["QD"][:, h, :], St[:, h, :], start=True, stop=False)
                    else:
                        for b in range(NB):
                            mm(B4(5)[0:n, h, :], m["QDM"][:, h, b, :], m["SS"][:, b, h, :],
                               start=b == 0, stop=False)
                    last = mm(B4(5)[0:n, h, :], m["DT"][0:n, h, :], m["VN"][0:n, h, :], start=False, stop=True)
                s(last, "o")
                if more:
                    gdn_v(t + 1, n)
                if n == P:
                    for h in range(H):
                        last = mm(B4(6)[:, h, :], m["KD"][:, h, :], m["VN"][:, h, :])
                    s(last, "ds")
                if more:
                    gdn_kk(t + 1, n)
                w("on")
                for h in range(H):
                    last = pe.transpose(B4(0)[:, h, 0:n], m["ON"][0:n, h, :], ident[0:n, 0:n])
                s(last, "oT")
                if n == NS:
                    for h in range(H):
                        pe.wait_ge(S("gs_vm"), h + 1)
                        if h:
                            pe.wait_ge(S("gs_new"), h)
                        for q in range(2):
                            last = mm(B[q][:, :], m["KD"][0:n, h, :],
                                      m["VNM"][0:n, 4 * q:4 * q + 4, :])
                        last.then_inc(S("gs_ds"), 1)

            def ml_prep():
                pe.wait_ge(S("mg_ready"), 1)
                for part, b0 in ((0, 0), (1, 3)):
                    for t in range(TILES + 1):
                        n = P if t < TILES else NS
                        last = pe.transpose(B[b0 + t // 4][0:H, (t % 4) * P:(t % 4) * P + n],
                                            cols[0:n, t, part, :], ident[0:n, 0:n])
                last.then_inc(S("m_rows"), 1)
                pe.wait_ge(S("m_rows_done"), 1)
                pe.wait_ge(S("m_lw_done"), 1)
                for t in range(TILES + 1):
                    n = P if t < TILES else NS
                    for q, r in enumerate((AR, LWR, MR)):
                        last = pe.transpose(B[6][0:n, t * 12 + 4 * q:t * 12 + 4 * q + 4],
                                            r[0:H, t * P:t * P + n], ident[0:H, 0:H])
                last.then_inc(S("m_cols"), 1)
                for h in range(H):
                    last = mm(B[7][:, h * 2 * NB:(h + 1) * 2 * NB], sel[:, h, :], KPR[0:H, :])
                last.then_inc(S("m_cols"), 1)

            def ml(t, n, k=0, xin=None):
                m = ml_map(n, k)
                X = m["X"]
                w = lambda name, v=None: pe.wait_ge(S("g_" + name), t + (1 + TILES + 1) if v is None else v)
                s = lambda ins, name: ins.then_inc(S("g_" + name), 1)
                pe.wait_ge(S(f"m_xin{k}"), xin)
                for h in range(H):
                    last = mm(B4(2)[0:n, h, 0:n], X[:, 4 + h, :], X[:, h, :])
                s(last, "kq")
                for h in range(H):
                    last = pe.transpose(B4(3)[0:n, h, :], X[:, 4 + h, :], ident[:, :])
                s(last, "kT")
                w("gr")
                for h in range(H):
                    last = mm(B4(0)[0:n, h, 0:n], sel[:, h, 0:n], rows4[:, 0, 0:n])
                s(last, "bc")
                for h in range(H):
                    last = mm(B4(1)[:, h, 0:n], sel[:, h, :], rows4[:, 1, 0:n])
                s(last, "bcW")
                for c in range(8):
                    last = pe.transpose(B4(4 + c // 4)[0:n, c % 4, :], X[:, 8 + c, :], ident[:, :])
                s(last, "vT")
                w("vb")
                w("qk")
                w("qd")
                w("DTe")
                w("E")
                for h in range(H):
                    bank = B[(0, 1, 6, 7)[h]]
                    if n == P:
                        w("state")
                        mm(bank[0:n, 0:DV + 1], m["QD"][:, h, :], CN[:, h, :], start=True, stop=False)
                    else:
                        pe.wait_ge(S(f"ms_cin{h % 2}"), 32 * (h // 2 + 1))
                        for b in range(NB):
                            mm(bank[0:n, 0:DV + 1], m["QDM"][:, h, b, :], m["CS2"][:, h % 2, b, :],
                               start=b == 0, stop=False)
                    last = mm(bank[0:n, 0:DV + 1], m["ST"][0:n, h, :], m["V1"][0:n, h, :],
                              start=False, stop=True)
                    if n == NS:
                        last.then_inc(S("ms_num"), 1)
                        pe.wait_ge(S("ms_vm"), h + 1)
                        w("rhs")
                        for b in range(NB):
                            if h * NB + b >= 4:
                                pe.wait_ge(S("ms_upd"), h * NB + b - 3)
                            mm(B[2 + b % 4][:, 0:DV + 1], m["KW"][0:n, h, :], m["VM"][0:n, b, :])\
                                .then_inc(S("ms_dc"), 1)
                if n == P:
                    s(last, "num")
                    w("rhs")
                    for h in range(H):
                        last = mm(B[2 + h][:, 0:DV + 1], m["KW"][:, h, :], m["V1"][:, h, :])
                    s(last, "ds")
                w("on")
                if n == P:
                    w("state", t + (TILES + 3))
                for half in range(2):
                    for h in range(H):
                        last = pe.transpose(B4(4 + half)[:, h, 0:n], m["HN"][0:n, h, half * P:(half + 1) * P],
                                            ident[0:n, 0:n])
                    s(last, ("z", "oT")[half])

            def store_y():
                pe.wait_ge(S("x_ready"), 4 * KT)
                pe.wait_ge(S("x_share"), 4 * KT)
                for t in range(TILES + 1):
                    n = P if t < TILES else NS
                    for q in range(2):
                        b = (2 * t + q) % 4
                        if 2 * t + q >= 4:
                            pe.wait_ge(S("y_copied"), 2 * t + q - 3)
                        for c in range(4):
                            last = pe.transpose(B[b][0:n, c * P:(c + 1) * P], xT[:, 4 * q + c, t * P:t * P + n],
                                                ident[:, :])
                        last.then_inc(S("x_turned"), 1)

            load_x()
            for l in range(2):
                phase_end(pe, "pe")
                norm(4 * l)
                if l == 0:
                    for c in range(NCONV):
                        if c == 0:
                            pe.wait_ge(S("wg_loaded"), 32)
                        last = pe.transpose(B[7][:, c * 24:(c + 1) * 24], cs_tm[0:24, c * P:(c + 1) * P],
                                            ident[0:24, 0:24])
                    last.then_inc(S("cs_T"), 1)
                linear(U0[l], AE0[l], NCH // 2, KT * 2 * l)
                gate_cols(l)
                if l == 0:
                    conv_tails()
                gate_turn(l)
                phase_end(pe, "pe")
                if l == 0:
                    gdn_prep()
                    phase_end(pe, "pe")
                    gdn_sums(0, P)
                    gdn_decays(0, P)
                    gdn_v(0, P)
                    gdn_kk(0, P)
                    with pe.Fori(0, TILES - 1) as t:
                        gdn(t, P, LEVELS, lambda v: t * (2 * LEVELS) + v, more=True)
                    gdn(TILES - 1, P, LEVELS, lambda v: (TILES - 1) * 2 * LEVELS + v)
                    phase_end(pe, "pe")
                    gdn_sums(TILES, NS)
                    gdn_decays(TILES, NS)
                    gdn_v(TILES, NS)
                    gdn_kk(TILES, NS)
                    gdn(TILES, NS, LEVELS_S, lambda v: TILES * 2 * LEVELS + v)
                else:
                    ml_prep()
                    phase_end(pe, "pe")
                    with pe.Fori(0, TILES // 2) as i:
                        for k in range(2):
                            ml(i * 2 + k, P, k, i * 16 + 16)
                    phase_end(pe, "pe")
                    ml(TILES, NS, 0, 16 * (TILES // 2 + 1))
                phase_end(pe, "pe")
                linear(U0[l] + U_IN, AE0[l] + J_IN, KT // 2)
                norm(4 * l + 1)
                norm(4 * l + 2)
                phase_end(pe, "pe", wait=False)
                ff(l)
                phase_end(pe, "pe")
                norm(4 * l + 3)
            phase_end(pe, "pe")
            store_y()

        @block.scalar
        def _(act):
            A_ = act.activation

            def hi(u, k):
                act.wait_ge(S("w_used"), u + 1)
                act.wait_ge(S(f"w_loaded{k % 2}"), 8 * u + (16 - 8 * (k % 2)))
                A_(whi[:, k % 2, :], wst[:, k % 2, :], ACT.Copy).then_inc(S("w_hi"), 1)

            def norm_sq(nn, src, ready=None, squared=False):
                for c in range(0 if squared else KT):
                    if ready:
                        ready(c)
                    if c >= 2:
                        act.wait_ge(S("squares_added"), KT * nn + c - 1)
                    A_(sq2[:, c % 2], src[:, c], ACT.Square).then_inc(S("squared"), 1)
                act.wait_ge(S("sumsq"), nn + 1)
                for tg in range(TG):
                    A_(lnss[:, tg * N:(tg + 1) * N], B[tg][:, 0:N], ACT.Ln, bias=epsc[:, :],
                       scale=1.0 / D).then_inc(S("lnss"), 1)
                act.wait_ge(S("lnss"), TG * (nn + 1))
                A_(rstd[:, :], lnss[:, :], ACT.Exp, scale=-0.5).then_inc(S("rstd"), 1)

            def norm_hi(m):
                for c in range(KT):
                    act.wait_ge(S("h_full"), KT * m + c + 1)
                    A_(hhi[:, c], hf2[:, c % 2], ACT.Copy).then_inc(S("h_hi"), 1)

            def x_ready(l_posts):
                def wait(c):
                    if l_posts:
                        act.wait_ge(S("x_ready"), KT * (l_posts - 1) + c + 1)
                        act.wait_ge(S("x_share"), KT * (l_posts - 1) + c + 1)
                return wait

            def load_x():
                act.sem_inc(S("act_evac"), BANKS)
                act.wait_ge(S("par_T"), 1)
                A_(par[:, :], B[6][:, 0:P], ACT.Copy).then_inc(S("par_ready"), 1)

            def plain_unit(j0, k, s0, func):
                act.wait_ge(S("row_free"), s0)
                for tg in range(TG):
                    act.wait_ge(S("job_done"), j0 + tg + 1)
                    A_(pout2[:, k % 2, tg * N:(tg + 1) * N], B[(k % 2) * TG + tg][:, 0:N], func)\
                        .then_inc(S("act_evac"), 1)

            def in_proj(l):
                u0, j0 = U0[l], J0[l]
                if l == 0:
                    hi(0, 0)

                def evac(i, c0, k, func):
                    plain_unit(i * 6 + (j0 + (c0 + k) * TG), k, i * 2 + (l * NCH + c0 + k + 1), func)

                def conv(i, k):
                    j = i * 6 + (j0 + k * TG)
                    act.wait_ge(S("tails_ready"), i * 2 + (k + 1))
                    row = xc2[:, k]
                    for tg in range(TG):
                        act.wait_ge(S("job_done"), j + tg + 1)
                        b = B[k * TG + tg]
                        if tg < TG - 1:
                            A_(row[:, 3 + tg * N:3 + (tg + 1) * N], b[:, 0:N], ACT.Copy).then_inc(S("act_evac"), 1)
                        else:
                            r = NP - tg * N
                            A_(row[:, 3 + tg * N:3 + NP], b[:, 0:r], ACT.Copy)
                            A_(row[:, XC:XCW].rearrange("p (b s) -> p b s", b=NB)[:, :, 3:3 + LS],
                               b[:, r:N].rearrange("p (b s) -> p b s", b=NB), ACT.Copy)\
                                .then_inc(S("act_evac"), 1)
                    act.wait_ge(S("conv_done"), i * 2 + (k + 1))
                    act.wait_ge(S("row_free"), i * 2 + (k + 1))
                    A_(pout2[:, k], cy2[:, k], ACT.Silu).then_inc(S("conv_act"), 1)

                spans = [(0, 6, "conv"), (12, 2, ACT.Silu), (16, 4, ACT.Gelu)] if l == 0 else \
                    [(0, 8, ACT.Copy), (16, 4, ACT.Sigmoid)]
                for c0, iters, func in spans:
                    with act.Fori(0, iters) as i:
                        for k in range(2):
                            hi(i * 2 + (u0 + c0 + k + 1), (k + 1) % 2)
                            if func == "conv":
                                conv(i, k)
                            else:
                                evac(i, c0, k, func)

            def out_proj(l):
                u0, j0 = U0[l] + U_IN, J0[l] + J_IN
                with act.Fori(0, KT // 2) as i:
                    for k in range(2):
                        hi(i * 2 + (u0 + k + 1), (k + 1) % 2)
                        act.wait_ge(S("squares_added"), i * 2 + (KT * (4 * l + 1) + k - 1))
                        for tg in range(TG):
                            act.wait_ge(S("job_done"), i * 6 + (j0 + k * TG + tg + 1))
                            last = A_(sq2[:, k, tg * N:(tg + 1) * N], B[k * TG + tg][:, 0:N], ACT.Square)
                            if tg == TG - 1:
                                last.then_inc(S("squared"), 1)
                            A_(accd(i * 2 + k, tg), B[k * TG + tg][:, 0:N].unsqueeze(1), ACT.Copy)\
                                .then_inc(S("act_evac"), 1)

            def ff_group(l, g, last):
                u0 = U0[l] + U_IN + U_OUT
                j0 = J0[l] + J_IN + J_OUT
                q0 = l * FG * J_W1
                for k in range(FK):
                    hi(g * (2 * FK) + (u0 + k + 1), (k + 1) % 2)
                    for tg in range(TG):
                        j = k * TG + tg
                        act.wait_ge(S("job_done"), g * (J_W1 + J_W2) + (j0 + j + 1))
                        act.wait_ge(S("h1_split"), g * J_W1 + (q0 + j + 1))
                        A_(relu2[:, j % 2], B[j % BANKS][:, 0:N], ACT.Relu).then_inc(S("act_evac"), 1)
                        act.wait_ge(S("act_evac"), g * J_W1 + (AE0[l] + J_IN + J_OUT + BANKS + j + 1))
                        A_(h1hi[:, k, tg * N:(tg + 1) * N], relu2[:, j % 2], ACT.Square)\
                            .then_inc(S("h1_hi"), 1)
                for k in range(FK):
                    if not (last and k == FK - 1):
                        hi(g * (2 * FK) + (u0 + FK + k + 1), (k + 1) % 2)

            def gdn_prep():
                act.wait_ge(S("gates_sb"), 1)
                gv = gates[:, :, :]
                A_(cols[:, :, 1, :], gv[:, :, 0:4], ACT.Sigmoid).then_inc(S("gexp"), 1)
                act.wait_ge(S("hvec_loaded"), 32)
                A_(hvec[:, 2, :], hvec[:, 0, :], ACT.Exp).then_inc(S("gexp"), 1)
                act.wait_ge(S("z_ready"), 1)
                z = gtmp[:, 0, :]
                A_(gtmp[:, 1, :], z, ACT.Abs).then_inc(S("gp"), 1)
                act.wait_ge(S("gp"), 1)
                A_(gtmp[:, 2, :], gtmp[:, 1, :], ACT.Exp, scale=-1.0).then_inc(S("gp"), 1)
                act.wait_ge(S("gp"), 2)
                A_(gtmp[:, 1, :], gtmp[:, 2, :], ACT.Ln, bias=1.0).then_inc(S("gp"), 1)
                act.wait_ge(S("gc_ready"), 1)
                A_(cols[:, :, 2, :], cols[:, :, 0, :], ACT.Exp).then_inc(S("gexp"), 1)
                act.wait_ge(S("gc_ready"), 2)
                A_(cols[:, :, 3, :], cols[:, :, 3, :], ACT.Exp).then_inc(S("gexp"), 1)
                A_(cols[:, 0:TILES, 4, :], B[7][:, 36:68].rearrange("p (t h) -> p t h", h=H), ACT.Exp)\
                    .then_inc(S("gexp"), 1)
                A_(keepb[:, 0:2, :].rearrange("p a b -> p (a b)"), B[7][:, 72:104], ACT.Exp)\
                    .then_inc(S("gexp"), 1)
                act.wait_ge(S("gc_rows"), 1)
                for q in range(2):
                    A_(GR[0:H, q * 512:(q + 1) * 512], B[q][0:H, :], ACT.Copy)
                A_(GR[0:H, NP:T], B[2][0:H, 0:NS], ACT.Copy)

            def rms_cols(t, n):
                act.wait_ge(S("g_oss"), t + 1)
                A_(small[0:n, 4, :], small[0:n, 3, :], ACT.Ln, bias=epsc[0:n, :], scale=1.0 / P)\
                    .then_inc(S("g_ossl"), 1)

            def rms_exp(t, n):
                act.wait_ge(S("g_ossl"), t + 1)
                A_(small[0:n, 5, :], small[0:n, 4, :], ACT.Exp, scale=-0.5).then_inc(S("g_ossr"), 1)

            def gdn_squares(t, n):
                m = gdn_map(n)
                A_(rows4[:, 0, 0:n], GR[0:H, bass.ds(t * P, n)], ACT.Copy).then_inc(S("g_gr"), 1)
                act.wait_ge(S("g_xin"), (t + 1) * 32)
                A_(m["SQ"], m["X"][:, 0:8, :], ACT.Square).then_inc(S("g_sq"), 1)

            def gdn_rms(t, n, end=None):
                m = gdn_map(n)
                w = lambda name: act.wait_ge(S("g_" + name), t + 1)
                s = lambda ins, name: ins.then_inc(S("g_" + name), 1)
                w("ss")
                A_(m["RB"][:, 0:4], B4(0)[:, :, 0:n], ACT.Ln, bias=epsc[:, :])
                s(A_(m["RB"][:, 4:8], B4(1)[:, :, 0:n], ACT.Ln, bias=epsc[:, :]), "ln")
                if end is not None:
                    out_squares(end, n)
                    rms_cols(end, n)
                w("vsT")
                for g in range(H):
                    last = A_(m["VB"][0:n, g, :], B4(7)[0:n, g, :], ACT.Square, accum_out=small[0:n, 0, g:g + 1])
                s(last, "vss")
                w("vss")
                s(A_(small[0:n, 1, :], small[0:n, 0, :], ACT.Ln, bias=epsc[0:n, :], scale=1.0 / P), "vssl")
                w("ln")
                s(A_(m["RB"], m["RB"], ACT.Exp, scale=-0.5), "rb")
                if end is not None:
                    rms_exp(end, n)
                w("bc")
                s(A_(m["E"], B4(2)[:, :, 0:n], ACT.Exp), "E")
                w("vssl")
                s(A_(small[0:n, 2, :], small[0:n, 1, :], ACT.Exp, scale=-0.5), "vssr")
                w("du")
                s(A_(m["Dm"][0:n], m["Dm"][0:n], ACT.Exp, scale=-1.0), "D")

            def out_squares(t, n):
                m = gdn_map(n)
                act.wait_ge(S("g_o"), t + 1)
                for h in range(H):
                    last = A_(m["ON"][0:n, h, :], B4(5)[0:n, h, :], ACT.Square, accum_out=small[0:n, 3, h:h + 1])
                last.then_inc(S("g_oss"), 1)

            def gdn(t, n, more=False):
                m = gdn_map(n)
                X = m["X"]
                w = lambda name, v=None: act.wait_ge(S("g_" + name), t + 1 if v is None else v)
                s = lambda ins, name: ins.then_inc(S("g_" + name), 1)
                w("dtu")
                s(A_(m["DT"][0:n], m["DT"][0:n], ACT.Exp), "DTe")
                w("vssr")
                for g in range(H):
                    last = A_(m["VB"][0:n, g, :], B4(7)[0:n, g, :], ACT.Copy, scale=small[0:n, 2, g:g + 1])
                s(last, "vsr")
                w("tc")
                w("kT")
                w("vT")
                for h in range(H):
                    A_(m["RW"][0:n, h, :], B4(5)[0:n, h, :], ACT.Copy, scale=tcol[0:n, 2, h:h + 1])
                    A_(m["KD"][0:n, h, :], B4(5)[0:n, h, :], ACT.Copy, scale=tcol[0:n, 3, h:h + 1])
                    last = A_(m["RU"][0:n, h, :], B4(6)[0:n, h, :], ACT.Copy, scale=tcol[0:n, 1, h:h + 1])
                s(last, "rhs")
                w("ofb")
                s(A_(hhi[:, 4:8, bass.ds(t * P, n)], m["OF"][:, 4:8], ACT.Copy), "hib")
                if more:
                    w("qd")
                    gdn_squares(t + 1, n)
                w("w")
                w("qn")
                s(A_(m["NW"], B4(3)[:, :, 0:n], ACT.Copy, scale=-1.0), "nw" if n == P else "nws")
                w("vnew")
                s(A_(m["VN"][0:n], B4(4)[0:n], ACT.Copy), "vns")
                if more:
                    gdn_rms(t + 1, n, end=t)
                else:
                    out_squares(t, n)
                    rms_cols(t, n)
                    rms_exp(t, n)
                w("ofa")
                s(A_(hhi[:, 0:4, bass.ds(t * P, n)], m["OF"][:, 0:4], ACT.Copy), "hi")

            def ml_prep():
                act.wait_ge(S("z_ready"), 2)
                z = gtmp[:, 0, :]
                A_(gtmp[:, 1, :], z, ACT.Abs).then_inc(S("mp"), 1)
                act.wait_ge(S("mp"), 1)
                A_(gtmp[:, 2, :], gtmp[:, 1, :], ACT.Exp, scale=-1.0).then_inc(S("mp"), 1)
                act.wait_ge(S("mp"), 2)
                A_(gtmp[:, 1, :], gtmp[:, 2, :], ACT.Ln, bias=1.0).then_inc(S("mp"), 1)
                act.wait_ge(S("m_rows"), 1)
                for b0, dst in ((0, IR), (3, LF)):
                    for q in range(2):
                        A_(dst[0:H, q * 512:(q + 1) * 512], B[b0 + q][0:H, :], ACT.Copy)
                    A_(dst[0:H, NP:T], B[b0 + 2][0:H, 0:NS], ACT.Copy).then_inc(S("m_rows_sb"), 1)
                act.wait_ge(S("m_keep_in"), 1)
                A_(KPR[0:H, :], KPR[0:H, :], ACT.Exp).then_inc(S("m_rows_done"), 1)
                act.wait_ge(S("m_cols"), 1)
                for q, (lo_, func, sc) in enumerate(((0, ACT.Copy, 1.0), (4, ACT.Exp, 1.0), (8, ACT.Exp, -1.0))):
                    A_(cum[:, 0:TILES, lo_:lo_ + 4],
                       B[6][:, 0:96].rearrange("p (t c) -> p t c", c=12)[:, :, lo_:lo_ + 4], func, scale=sc)
                    A_(cum[0:NS, TILES, lo_:lo_ + 4], B[6][0:NS, 96 + lo_:100 + lo_], func, scale=sc)
                act.wait_ge(S("m_cols"), 2)
                A_(keepb[:, :, :].rearrange("p a b -> p (a b)"), B[7][:, 0:H * 2 * NB], ACT.Copy)

            def ml(t, n, k=0, xin=None):
                m = ml_map(n, k)
                w = lambda name, v=None: act.wait_ge(S("g_" + name), t + (1 + TILES + 1) if v is None else v)
                s = lambda ins, name: ins.then_inc(S("g_" + name), 1)
                A_(rows4[:, 0, 0:n], ROWM[0:H, bass.ds(t * P, n)], ACT.Copy)
                s(A_(rows4[:, 1, 0:n], ROWW[0:H, bass.ds(t * P, n)], ACT.Copy), "gr")
                w("bcW", t + 1)
                s(A_(m["E"], B4(1)[:, :, 0:n], ACT.Exp), "E")
                w("dtu")
                s(A_(m["WTm"][0:n], m["WTm"][0:n], ACT.Exp), "DTe")
                w("vT")
                for q in range(2):
                    last = A_(m["V1"][0:n, 2 * q:2 * q + 2, 0:DV],
                              B[4 + q][0:n, :].rearrange("p (h v) -> p h v", h=2), ACT.Copy)
                s(last, "vb")
                for h in range(H):
                    if n == NS:
                        act.wait_ge(S("ms_num"), h + 1)
                    elif h == 0:
                        w("num", t + 1)
                    bank = B[(0, 1, 6, 7)[h]]
                    A_(small[0:n, 1, h:h + 1], bank[0:n, DV:DV + 1], ACT.Abs)
                    last = A_(m["HN"][0:n, h], bank[0:n, 0:DV], ACT.Square, accum_out=small[0:n, 0, h:h + 1])
                s(last, "oss")
                w("ms", t + 1)
                s(A_(small[0:n, 4, :], small[0:n, 3, :], ACT.Ln, bias=epsc[0:n, :], scale=1.0 / DV), "ossl")
                w("ossl")
                s(A_(small[0:n, 5, :], small[0:n, 4, :], ACT.Exp, scale=-0.5), "ossr")
                w("ofa")
                w("ofb")
                s(A_(hhi[:, :, bass.ds(t * P, n)], m["OF"], ACT.Copy), "hi")

            def store_y():
                for t in range(TILES + 1):
                    n = P if t < TILES else NS
                    for q in range(2):
                        act.wait_ge(S("x_turned"), 2 * (TILES + 1) + 2 * t + q + 1)
                        if t >= 2:
                            act.wait_ge(S(f"y_stored{t % 2}"), 16 * (t // 2))
                        A_(x_tm[0:n, t % 2, q * 512:(q + 1) * 512], B[(2 * t + q) % 4][0:n, :], ACT.Copy)\
                            .then_inc(S("y_copied"), 1)

            load_x()
            phase = lambda: phase_end(act, "act")
            for l in range(2):
                phase()
                norm_sq(4 * l, xT, x_ready(2 * l))
                norm_hi(2 * l)
                if l == 0:
                    act.wait_ge(S("cs_T"), 1)
                    A_(csT.rearrange("p a b -> p (a b)"), B[7][:, 0:NCONV * 24], ACT.Copy).then_inc(S("csT_ready"), 1)
                act.wait_ge(S("wg_loaded"), 16 * (2 + 2 * l))
                A_(wg_hi[:, :, :], wg[:, :, :], ACT.Copy).then_inc(S("wg_hi_ready"), 1)
                in_proj(l)
                act.wait_ge(S("gate_rows"), l + 1)
                for tg in range(TG):
                    last = A_(gT[0:2 * H, tg * N:(tg + 1) * N], B[(6, 7, 3)[tg]][0:2 * H, 0:N], ACT.Copy)
                last.then_inc(S("gate_rows_sb"), 1)
                if l == 0:
                    act.wait_ge(S("tails_T"), 1)
                    for q in range(3):
                        last = A_(tail_tm[0:27, q * 512:(q + 1) * 512], B[q][0:27, :], ACT.Copy)
                    last.then_inc(S("tails_sb"), 1)
                act.wait_ge(S("gates_done"), l + 1)
                if l == 0:
                    act.wait_ge(S("cols_zero"), 1)
                A_(gates[:, 0:TILES, :], B[4][:, 0:64].rearrange("p (t c) -> p t c", c=8), ACT.Copy)
                A_(gates[0:NS, TILES, :], B[4][0:NS, 64:72], ACT.Copy).then_inc(S("gates_sb"), 1)
                phase()
                if l == 0:
                    gdn_prep()
                    phase()
                    gdn_squares(0, P)
                    gdn_rms(0, P)
                    with act.Fori(0, TILES - 1) as t:
                        gdn(t, P, more=True)
                    gdn(TILES - 1, P)
                    phase()
                    gdn_squares(TILES, NS)
                    gdn_rms(TILES, NS)
                    gdn(TILES, NS)
                else:
                    ml_prep()
                    phase()
                    with act.Fori(0, TILES // 2) as i:
                        for k in range(2):
                            ml(i * 2 + k, P, k, i * 16 + 16)
                    phase()
                    ml(TILES, NS, 0, 16 * (TILES // 2 + 1))
                phase()
                out_proj(l)
                norm_sq(4 * l + 1, acc, squared=True)
                norm_sq(4 * l + 2, xT, x_ready(2 * l + 1))
                norm_hi(2 * l + 1)
                phase()
                with act.Fori(0, FG - 1) as g:
                    ff_group(l, g, False)
                ff_group(l, FG - 1, l == 1)
                phase()
                norm_sq(4 * l + 3, acc)
            phase()
            store_y()

        @block.vector
        def _(dve):
            def lo(u, k):
                dve.wait_ge(S("w_hi"), u + 1)
                dve.tensor_tensor(wlo[:, k % 2, :], wst[:, k % 2, :], whi[:, k % 2, :].bitcast(F32),
                                  ALU.subtract).then_inc(S("w_split"), 1)

            def add_squares(nn):
                for c in range(KT):
                    dve.wait_ge(S("squared"), KT * nn + c + 1)
                    if c == 0:
                        ins = dve.tensor_copy(ssum[:, :], sq2[:, 0])
                    else:
                        dve.wait_ge(S("squares_added"), KT * nn + c)
                        ins = dve.tensor_tensor(ssum[:, :], ssum[:, :], sq2[:, c % 2], ALU.add)
                    ins.then_inc(S("squares_added"), 1)

            def gain(l, q, c):
                return par[:, (l * 4 + q) * KT + c:(l * 4 + q) * KT + c + 1]

            def pre_norm(nn, m):
                add_squares(nn)
                l, q = nn // 4, nn % 4
                dve.wait_ge(S("rstd"), nn + 1)
                dve.wait_ge(S("par_ready"), 1)

                def rest(c):
                    dve.wait_ge(S("h_hi"), KT * m + c + 1)
                    dve.tensor_tensor(hlo[:, c], hf2[:, c % 2], hhi[:, c].bitcast(F32), ALU.subtract)\
                        .then_inc(S("h_split"), 1)
                for c in range(KT):
                    if c >= 2:
                        dve.wait_ge(S("h_split"), KT * m + c - 1)
                    dve.scalar_tensor_tensor(hf2[:, c % 2], xT[:, c], gain(l, q, c), rstd[:, :], ALU.mult,
                                             ALU.mult).then_inc(S("h_full"), 1)
                    if c:
                        rest(c - 1)
                rest(KT - 1)

            def post_norm(nn, added=False):
                if not added:
                    add_squares(nn)
                l, q = nn // 4, nn % 4
                p = nn // 2

                def share(c):
                    dve.wait_ge(S("mix_normed"), KT * p + c + 1)
                    dve.tensor_tensor(xT[:, c, 0:RS], xT[:, c, 0:RS], hf2[:, c % 2, 0:RS], ALU.add)\
                        .then_inc(S("x_share"), 1)
                dve.wait_ge(S("rstd"), nn + 1)
                for c in range(KT):
                    if c >= 2:
                        dve.wait_ge(S("x_ready"), KT * p + c - 1)
                        dve.wait_ge(S("x_share"), KT * p + c - 1)
                    dve.scalar_tensor_tensor(hf2[:, c % 2], acc[:, c], gain(l, q, c), rstd[:, :], ALU.mult,
                                             ALU.mult).then_inc(S("mix_normed"), 1)
                    if c:
                        share(c - 1)
                share(KT - 1)

            def load_x():
                dve.sem_inc(S("dve_evac"), BANKS)
                dve.sem_inc(S("w_split"), 2)
                dve.sem_inc(S("tails_ready"), 2)
                dve.sem_inc(S("h1_split"), 2)
                dve.sem_inc(S("xT_copied"), 4)
                dve.memset(epsc[:, :], EPS)
                with dve.Fori(0, TILES // 2) as i:
                    for k in range(2):
                        for q in range(2):
                            dve.wait_ge(S("x_turned"), i * 4 + (2 * k + q + 1))
                            dve.tensor_copy(xT[:, 4 * q:4 * q + 4, bass.ds(i * (2 * P) + k * P, P)],
                                            B4(2 * k + q)).then_inc(S("xT_copied"), 1)
                for q in range(2):
                    dve.wait_ge(S("x_turned"), 2 * TILES + q + 1)
                    dve.tensor_copy(xT[:, 4 * q:4 * q + 4, NP:T],
                                    B[q][:, 0:4 * NS].rearrange("p (c n) -> p c n", c=4)).then_inc(S("xT_copied"), 1)

            def conv_block(i, k):
                cw = cw2[:, k]
                c = i * 2 + k
                for j in range(CONVW):
                    dve.tensor_copy(cw[:, j:j + 1], par[:, bass.ds(c + (64 + j * NCONV), 1)])
                row, y = xc2[:, k], cy2[:, k]
                smp = row[:, XC:XCW].rearrange("p (b s) -> p b s", b=NB)
                dve.tensor_copy(smp[:, :, 0:3], csT[:, bass.ds(c, 1), :].rearrange("p a (b s) -> p (a b) s", s=3))\
                    .then_inc(S("taps"), 1)
                dve.wait_ge(S("taps"), i * 2 + (k + 1))
                dve.wait_ge(S("act_evac"), i * 6 + (BANKS + (k + 1) * TG))
                dve.wait_ge(S("conv_act"), i * 2 + (k + 1))
                ys = y[:, NP:T].rearrange("p (b s) -> p b s", b=NB)
                for j in range(CONVW):
                    parts = ((y[:, 0:NP], row[:, j:j + NP]), (ys, smp[:, :, j:j + LS]))
                    if j:
                        dve.wait_ge(S("tap"), i * 8 + (4 * k + j))
                    for o, x in parts:
                        if j == 0:
                            ins = dve.tensor_scalar(o, x, cw[:, 0:1], None, ALU.mult)
                        else:
                            ins = dve.scalar_tensor_tensor(o, x, cw[:, j:j + 1], o, ALU.mult, ALU.add)
                    ins.then_inc(S("tap"), 1)
                dve.wait_ge(S("tap"), i * 8 + (4 * k + 4))
                dve.tensor_copy(tails[:, bass.ds(c, 1), 0:3], row[:, NP:NP + 3].unsqueeze(1))\
                    .then_inc(S("conv_done"), 1)
                dve.tensor_copy(tails[:, bass.ds(c, 1), 3:27].rearrange("p a (b s) -> p (a b) s", s=3),
                                smp[:, :, LS:LS + 3]).then_inc(S("tails_ready"), 1)

            def in_proj(l):
                u0 = U0[l]
                if l == 0:
                    dve.memset(xc2[:, :, 0:3], 0.0)
                    dve.wait_ge(S("csT_ready"), 1)
                    lo(0, 0)
                    with dve.Fori(0, 6) as i:
                        for k in range(2):
                            lo(i * 2 + (k + 1), (k + 1) % 2)
                            conv_block(i, k)
                    dve.wait_ge(S("tails_ready"), 2 + NCONV)
                    dve.wait_ge(S("conv_act"), 2 + NCONV)
                    dve.memset(WTS[0:NS], 0.0).then_inc(S("filled"), 1)
                    with dve.Fori(0, 6) as i:
                        for k in range(2):
                            lo(i * 2 + (12 + k + 1), (k + 1) % 2)
                else:
                    with dve.Fori(0, NCH // 2) as i:
                        for k in range(2):
                            lo(i * 2 + (u0 + k + 1), (k + 1) % 2)

            def ff_group(l, g, last):
                u0 = U0[l] + U_IN + U_OUT
                j0 = J0[l] + J_IN + J_OUT
                q0 = l * FG * J_W1
                for k in range(FK):
                    lo(g * (2 * FK) + (u0 + k + 1), (k + 1) % 2)
                    for tg in range(TG):
                        j = k * TG + tg
                        dve.wait_ge(S("h1_hi"), g * J_W1 + (q0 + j + 1))
                        dve.tensor_tensor(relu2[:, j % 2], relu2[:, j % 2], relu2[:, j % 2], ALU.mult)\
                            .then_inc(S("h1_sq"), 1)
                        dve.wait_ge(S("h1_sq"), g * J_W1 + (q0 + j + 1))
                        dve.tensor_tensor(h1lo[:, k, tg * N:(tg + 1) * N], relu2[:, j % 2],
                                          h1hi[:, k, tg * N:(tg + 1) * N].bitcast(F32), ALU.subtract)\
                            .then_inc(S("h1_split"), 1)
                for k in range(FK):
                    if not (last and k == FK - 1):
                        lo(g * (2 * FK) + (u0 + FK + k + 1), (k + 1) % 2)
                    for oc in range(2):
                        for tg in range(TG):
                            j = (2 * k + oc) * TG + tg
                            a = acc[:, 2 * k + oc, tg * N:(tg + 1) * N]
                            dve.wait_ge(S("job_done"), g * (J_W1 + J_W2) + (j0 + J_W1 + j + 1))
                            dve.tensor_tensor(a, B[j % BANKS][:, 0:N], a, ALU.add).then_inc(S("dve_evac"), 1)

            def bcl(ap, shape):
                return ap.unsqueeze(2).broadcast_to(shape)

            def bcm(ap, shape):
                return ap.unsqueeze(1).broadcast_to(shape)

            TT, STT = dve.tensor_tensor, dve.scalar_tensor_tensor

            def gdn_prep():
                dve.wait_ge(S("gates_sb"), 1)
                dve.wait_ge(S("hvec_loaded"), 32)
                z = gtmp[:, 0, :].rearrange("p (t h) -> p t h", h=H)
                TT(z, gates[:, :, 4:8], bcm(hvec[:, 1, :], [P, TILES + 1, H]), ALU.add).then_inc(S("z_ready"), 1)
                dve.wait_ge(S("gp"), 3)
                STT(gtmp[:, 2, :], gtmp[:, 0, :], 0.0, gtmp[:, 1, :], ALU.max, ALU.add).then_inc(S("gq"), 1)
                dve.wait_ge(S("gq"), 1)
                dve.wait_ge(S("gexp"), 2)
                STT(cols[:, :, 5, :], gtmp[:, 2, :].rearrange("p (t h) -> p t h", h=H), -1.0,
                    bcm(hvec[:, 2, :], [P, TILES + 1, H]), ALU.mult, ALU.mult).then_inc(S("cols_g"), 1)
                dve.wait_ge(S("cols_g"), 1)
                TT(gtmp[0:NS, 3, 0:32].rearrange("p (b h) -> p b h", h=H), bcm(cols[0:NS, TILES, 5, :], [NS, NB, H]),
                   bcl(rowmask[:, :], [NS, NB, H]), ALU.mult).then_inc(S("cols_g"), 1)
                dve.wait_ge(S("cum_done"), 1)
                dve.wait_ge(S("cols_zero"), 1)
                dve.tensor_copy(cols[:, 0:TILES, 0, :], B[7][:, 0:32].rearrange("p (t h) -> p t h", h=H))
                dve.tensor_copy(cols[0:NS, TILES, 0, :], B[7][0:NS, 32:36]).then_inc(S("gc_ready"), 1)
                dve.wait_ge(S("gc_ready"), 1)
                TT(cols[:, 0:TILES, 3, :], B[7][:, 36:68].rearrange("p (t h) -> p t h", h=H),
                   cols[:, 0:TILES, 0, :], ALU.subtract)
                TT(cols[0:NS, TILES, 3, :], B[7][0:NS, 68:72], cols[0:NS, TILES, 0, :], ALU.subtract)\
                    .then_inc(S("gc_ready"), 1)
                dve.wait_ge(S("gexp"), 6)
                TT(cols[:, :, 2, :], cols[:, :, 2, :], cols[:, :, 1, :], ALU.mult)
                dve.wait_ge(S("sgw_T"), 1)
                TT(WT[:, :, :], B4(3), bcm(triU[:, :], [P, H, P]), ALU.mult)
                TT(WTS[0:NS], B[4][0:NS, 0:H * NS].rearrange("p (g n) -> p g n", g=H), bcm(triUS[:, :], [NS, H, NS]),
                   ALU.mult)
                dve.memset(St[:, :, :], 0.0).then_inc(S("g_state"), 1)

            def gdn_keys(t, n):
                m = gdn_map(n)
                dve.tensor_copy(tcol[0:n].unsqueeze(1), cols[0:n, bass.ds(t, 1)]).then_inc(S("g_tc"), 1)
                for q in range(2):
                    last = dve.tensor_copy(m["XX"][0:n, q], bcm(ident[0:n, 0:n], [n, 4, n]))
                last.then_inc(S("g_Xinit"), 1)
                dve.wait_ge(S("g_rb"), t + 1)
                TT(m["QH"][:, 4:8], m["X"][:, 4:8], m["RB"][:, 4:8], ALU.mult).then_inc(S("g_kn"), 1)

            def gdn_decay(t, n):
                m = gdn_map(n)
                mp = maskpos if n == P else maskposS
                dve.wait_ge(S("g_tc"), t + 1)
                dve.wait_ge(S("g_E"), t + 1)
                for h in range(H):
                    last = STT(m["Dm"][0:n, h], B4(2)[0:n, h, 0:n], tcol[0:n, 0, h:h + 1], mp[:, :],
                               ALU.subtract, ALU.add)
                last.then_inc(S("g_du"), 1)
                STT(m["QH"][:, 0:4], m["X"][:, 0:4], QSCALE, m["RB"][:, 0:4], ALU.mult, ALU.mult)\
                    .then_inc(S("g_qn"), 1)

            def gdn_decay_T(t, n):
                m = gdn_map(n)
                mn = masknegT if n == P else masknegTS
                for h in range(H):
                    last = STT(m["DT"][0:n, h], B4(2)[0:n, h, 0:n], tcol[0:n, 0, h:h + 1], mn[:, :],
                               ALU.subtract, ALU.add)
                last.then_inc(S("g_dtu"), 1)

            def gdn(t, n, lv, lv0, more=False):
                m = gdn_map(n)
                X, QH = m["X"], m["QH"]
                w = lambda name, v=None: dve.wait_ge(S("g_" + name), t + 1 if v is None else v)
                s = lambda ins, name: ins.then_inc(S("g_" + name), 1)
                beta, gl = tcol[0:n, 1, :], tcol[0:n, 4, :]
                w("D")
                w("kk")
                for h in range(H):
                    last = STT(m["A"][0:n, h], B4(3)[0:n, h, 0:n], beta[:, h:h + 1], m["Dm"][0:n, h],
                               ALU.mult, ALU.mult)
                s(last, "A")
                w("DTe")
                w("kq")
                s(TT(m["DT"][0:n], B4(4)[0:n, :, 0:n], m["DT"][0:n], ALU.mult), "qk")

                def beside(q):
                    if q == 0:
                        w("qn")
                        s(TT(m["QD"], QH[:, 0:4], m["E"], ALU.mult), "qd" if n == P else "qds")
                    if q == min(4, lv):
                        w("z")
                        dve.wait_ge(S("g_xgate"), (t + 1) * 16)
                        s(TT(m["OF"][:, 4:8], B4(3)[:, :, 0:n], X[:, 16:20], ALU.mult), "ofb")
                    if q == min(6, lv):
                        w("hib")
                        TT(hlo[:, 4:8, bass.ds(t * P, n)], m["OF"][:, 4:8],
                           hhi[:, 4:8, bass.ds(t * P, n)].bitcast(F32), ALU.subtract)

                for q in range(lv):
                    for p in range(2):
                        w("t2", lv0(2 * q + 1 + p))
                        s(TT(m["T2"][0:n, 2 * p:2 * p + 2], B4((0, 7)[p])[0:n, 0:2, 0:n],
                             bcm(lmask[0:n, q, 0:n], [n, 2, n]), ALU.mult), "t2s")
                    beside(q)
                    c0 = 2 if q == lv - 1 else 0
                    for p in range(2):
                        w("x", lv0(2 * q + 1 + p))
                        x = m["XX"][0:n, p, c0:4]
                        s(TT(x, x, B4(1 + p)[0:n, c0:4, 0:n], ALU.subtract), "inv")
                if n == NS:
                    w("qds", 1)
                    s(TT(m["QDM"], m["QD"].unsqueeze(2).broadcast_to([P, H, NB, NS]),
                         colmask[:, :, :].unsqueeze(1).broadcast_to([P, H, NB, NS]), ALU.mult), "qd")
                    beside(lv)
                if n == NS:
                    w("nws", 1)
                    s(TT(m["NWM"], m["NW"].unsqueeze(2).broadcast_to([P, H, NB, NS]),
                         colmask[:, :, :].unsqueeze(1).broadcast_to([P, H, NB, NS]), ALU.mult), "nw")
                w("o")
                if n == P:
                    s(TT(St[:, :, :], St[:, :, :], bcl(gl, [P, H, P]), ALU.mult), "sg")
                    w("sg")
                    w("ds")
                    s(TT(St[:, :, :], St[:, :, :], B4(6), ALU.add), "state")
                if more:
                    gdn_keys(t + 1, n)
                w("ossr")
                s(TT(m["ON"][0:n], B4(5)[0:n], bcl(small[0:n, 5, :], [n, H, P]), ALU.mult), "on")
                if more:
                    gdn_decay(t + 1, n)
                w("oT")
                s(STT(m["OF"][:, 0:4], B4(0)[:, :, 0:n], par[:, 112:113], X[:, 12:16], ALU.mult, ALU.mult), "ofa")
                if more:
                    gdn_decay_T(t + 1, n)
                w("hi")
                TT(hlo[:, 0:4, bass.ds(t * P, n)], m["OF"][:, 0:4], hhi[:, 0:4, bass.ds(t * P, n)].bitcast(F32),
                   ALU.subtract)
                if n == NS:
                    gls = keepb[:, 0:2, :].rearrange("p a (b h) -> p (a b) h", h=H)
                    for h in range(H):
                        if h:
                            dve.wait_ge(S("gs_ds"), h)
                        TT(m["VNM"][0:n], bcm(m["VN"][0:n, h], [n, NB, P]), bcl(rowmask[:, :], [n, NB, P]),
                           ALU.mult).then_inc(S("gs_vm"), 1)
                        TT(m["SS"][:, :, h], m["SS"][:, :, h], bcl(gls[:, :, h], [P, NB, P]), ALU.mult)\
                            .then_inc(S("gs_dec"), 1)
                        dve.wait_ge(S("gs_dec"), h + 1)
                        dve.wait_ge(S("gs_ds"), h + 1)
                        for q in range(2):
                            last = TT(m["SS"][:, 4 * q:4 * q + 4, h], m["SS"][:, 4 * q:4 * q + 4, h], B4(q), ALU.add)
                        last.then_inc(S("gs_new"), 1)

            def ml_prep():
                dve.wait_ge(S("gates_sb"), 2)
                dve.wait_ge(S("hvec_loaded"), 64)
                gb = hvec[:, 0:2, :]
                z = gtmp[:, 0, :].rearrange("p (t h) -> p t h", h=H)
                TT(cols[:, :, 0, :], gates[:, :, 0:4], bcm(gb[:, 0], [P, TILES + 1, H]), ALU.add)
                TT(z, gates[:, :, 4:8], bcm(gb[:, 1], [P, TILES + 1, H]), ALU.add).then_inc(S("z_ready"), 1)
                dve.wait_ge(S("mp"), 3)
                STT(cols[:, :, 1, :], z, 0.0, gtmp[:, 1, :].rearrange("p (t h) -> p t h", h=H), ALU.min,
                    ALU.subtract).then_inc(S("mg_ready"), 1)
                c = [0]

                def link(ins):
                    c[0] += 1
                    ins.then_inc(S("m_row_step"), 1)
                    dve.wait_ge(S("m_row_step"), c[0])

                def tiles(r):
                    return r[0:H, 0:NP].rearrange("p (t n) -> p t n", t=TILES)

                def seqs(r):
                    return r[0:H, NP:T].rearrange("p (b n) -> p b n", b=NB)

                link(dve.memset(RST[0:H, :], 1.0))
                dve.memset(tiles(RST)[:, :, 0:1], 0.0)
                link(dve.memset(seqs(RST)[:, :, 0:1], 0.0))
                dve.wait_ge(S("m_rows_sb"), 2)
                link(dve.tensor_tensor_scan(BR[0:H, :], RST[0:H, :], LF[0:H, :], 0.0, ALU.mult, ALU.add))
                link(dve.tensor_tensor_scan(MR[0:H, 0:NP], LF[0:H, 0:NP], IR[0:H, 0:NP], 0.0, ALU.add, ALU.max))
                dve.memset(D0X[0:H, :, 0:1], -BIG)
                dve.tensor_copy(D1X[0:H, :, 0:1], MPR[0:H, NB:2 * NB].unsqueeze(2))
                dve.tensor_copy(D0X[0:H, :, 1:], seqs(LF))
                link(dve.tensor_copy(D1X[0:H, :, 1:], seqs(IR)))
                flat = lambda r: r[0:H].rearrange("p b s -> p (b s)")
                link(dve.tensor_tensor_scan(flat(MSX), flat(D0X), flat(D1X), 0.0, ALU.add, ALU.max))
                link(dve.tensor_copy(seqs(MR), MSX[0:H, :, 1:]))
                dve.memset(MPR[0:H, 0:1], 0.0)
                dve.tensor_copy(MPR[0:H, 1:TILES].unsqueeze(2), tiles(MR)[:, 0:TILES - 1, P - 1:P])
                for dst, r in ((MLA, MR), (BLA, BR)):
                    dve.tensor_copy(dst[0:H, 0:TILES].unsqueeze(2), tiles(r)[:, :, P - 1:P])
                    last = dve.tensor_copy(dst[0:H, TILES:2 * NB].unsqueeze(2), seqs(r)[:, :, LS - 1:LS])
                link(last)
                TT(AR[0:H, :], IR[0:H, :], BR[0:H, :], ALU.subtract)
                TT(ROWM[0:H, :], BR[0:H, :], MR[0:H, :], ALU.subtract)
                link(TT(BLA[0:H, :], MLA[0:H, :], BLA[0:H, :], ALU.subtract))
                TT(KPR[0:H, :], MPR[0:H, :], BLA[0:H, :], ALU.subtract).then_inc(S("m_keep_in"), 1)
                for v, a, b in ((tiles, 0, TILES), (seqs, NB, 2 * NB)):
                    shape = [H, TILES, P] if v is tiles else [H, NB, LS]
                    TT(v(ROWW), v(ROWM), bcl(MPR[0:H, a:b], shape), ALU.add)
                    last = TT(v(LWR), v(AR), bcl(BLA[0:H, a:b], shape), ALU.subtract)
                link(last)
                dve.sem_inc(S("m_lw_done"), 1)
                dve.memset(CN[:, :, :], 0.0).then_inc(S("g_state"), 1)

            def ml(t, n, k=0, xin=None):
                m = ml_map(n, k)
                X = m["X"]
                w = lambda name, v=None: dve.wait_ge(S("g_" + name), t + (1 + TILES + 1) if v is None else v)
                s = lambda ins, name: ins.then_inc(S("g_" + name), 1)
                s(dve.tensor_copy(tcol[0:n, 0:3, :].rearrange("p a h -> p (a h)").unsqueeze(1),
                                  cum[0:n, bass.ds(t, 1)]), "tc")
                a, wk, em = (tcol[0:n, i, :] for i in range(3))
                if n == P:
                    s(dve.tensor_copy(small[:, 6, :].unsqueeze(2), keepb[:, :, bass.ds(t, 1)]), "tk")
                w("tc")
                w("kT")
                s(TT(m["KW"][0:n], B4(3)[0:n], bcl(wk, [n, H, P]), ALU.mult), "rhs")
                w("bc")
                mn = masknegT if n == P else masknegTS
                for h in range(H):
                    last = STT(m["WTm"][0:n, h], B4(0)[0:n, h, 0:n], a[:, h:h + 1], mn[:, :], ALU.add, ALU.add)
                s(last, "dtu")
                dve.wait_ge(S(f"m_xin{k}"), xin)
                w("E")
                s(STT(m["QD"], X[:, 0:4], QSCALE, m["E"], ALU.mult, ALU.mult), "qd" if n == P else "qds")
                if n == NS:
                    w("qds", 2)
                    s(TT(m["QDM"], m["QD"].unsqueeze(2).broadcast_to([P, H, NB, NS]),
                         colmask[:, :, :].unsqueeze(1).broadcast_to([P, H, NB, NS]), ALU.mult), "qd")
                w("kq")
                w("DTe")
                s(STT(m["ST"][0:n], B4(2)[0:n, :, 0:n], QSCALE, m["WTm"][0:n], ALU.mult, ALU.mult), "qk")
                if n == NS:
                    w("vb")
                    kp = keepb
                    for h in range(H):
                        if h:
                            dve.wait_ge(S("ms_dc"), h * NB)
                        TT(m["VM"][0:n], bcm(m["V1"][0:n, h], [n, NB, DV + 1]), bcl(rowmask[:, :], [n, NB, DV + 1]),
                           ALU.mult).then_inc(S("ms_vm"), 1)
                        for b in range(NB):
                            dve.wait_ge(S("ms_dc"), h * NB + b + 1)
                            cs = m["CS2"][:, h % 2, b, :]
                            STT(cs, cs, kp[:, h, TILES + b:TILES + b + 1], B[2 + b % 4][:, 0:DV + 1],
                                ALU.mult, ALU.add).then_inc(S("ms_upd"), 1)
                w("oss")
                s(TT(small[0:n, 1, :], small[0:n, 1, :], em, ALU.max), "den")
                w("den", t + 1)
                s(dve.reciprocal(small[0:n, 2, :], small[0:n, 1, :]), "rd")
                w("rd", t + 1)
                s(TT(small[0:n, 7, :], small[0:n, 0, :], small[0:n, 2, :], ALU.mult), "ms1")
                w("ms1", t + 1)
                s(TT(small[0:n, 3, :], small[0:n, 7, :], small[0:n, 2, :], ALU.mult), "ms")
                if n == P:
                    w("tk", t + 1)
                    w("ds", t + (TILES + 1))
                    for h in range(H):
                        last = STT(CN[:, h], CN[:, h], small[:, 6, h:h + 1], B[2 + h][:, 0:DV + 1],
                                   ALU.mult, ALU.add)
                    s(last, "state")
                w("ossr")
                s(TT(small[0:n, 7, :], small[0:n, 5, :], small[0:n, 2, :], ALU.mult), "f")
                w("f", t + 1)
                for h in range(H):
                    last = dve.tensor_scalar(m["HN"][0:n, h], B[(0, 1, 6, 7)[h]][0:n, 0:DV], small[0:n, 7, h:h + 1],
                                             None, ALU.mult)
                s(last, "on")
                for q in range(2):
                    w(("z", "oT")[q])
                    s(STT(m["OF"][:, q:8:2], B4(4 + q)[:, :, 0:n], par[:, 117 + q:118 + q], X[:, 16 + q:24:2],
                          ALU.mult, ALU.mult), ("ofa", "ofb")[q])
                w("hi")
                TT(hlo[:, :, bass.ds(t * P, n)], m["OF"], hhi[:, :, bass.ds(t * P, n)].bitcast(F32), ALU.subtract)

            phase = lambda: phase_end(dve, "dve")
            load_x()
            for l in range(2):
                phase()
                pre_norm(4 * l, 2 * l)
                if l == 0:
                    dve.memset(gates[:, :, :], 0.0)
                    dve.memset(cum[:, :, :], 0.0)
                    dve.memset(gtmp[:, :, :], 0.0)
                    dve.memset(cols[:, :, :, :], 0.0).then_inc(S("cols_zero"), 1)
                    dve.sem_inc(S("conv_act"), 2)
                dve.wait_ge(S("wg_hi_ready"), l + 1)
                dve.tensor_tensor(wg_lo[:, :, :], wg[:, :, :], wg_hi[:, :, :].bitcast(F32), ALU.subtract)\
                    .then_inc(S("wg_split"), 1)
                in_proj(l)
                phase()
                if l == 0:
                    gdn_prep()
                    phase()
                    gdn_keys(0, P)
                    gdn_decay(0, P)
                    gdn_decay_T(0, P)
                    with dve.Fori(0, TILES - 1) as t:
                        gdn(t, P, LEVELS, lambda v: t * (2 * LEVELS) + v, more=True)
                    gdn(TILES - 1, P, LEVELS, lambda v: (TILES - 1) * 2 * LEVELS + v)
                    phase()
                    gdn_keys(TILES, NS)
                    gdn_decay(TILES, NS)
                    gdn_decay_T(TILES, NS)
                    gdn(TILES, NS, LEVELS_S, lambda v: TILES * 2 * LEVELS + v)
                else:
                    ml_prep()
                    phase()
                    with dve.Fori(0, TILES // 2) as i:
                        for k in range(2):
                            ml(i * 2 + k, P, k, i * 16 + 16)
                    phase()
                    dve.memset(ml_map(NS)["V1"][0:NS, :, DV:DV + 1], 1.0).then_inc(S("filled"), 1)
                    dve.wait_ge(S("filled"), 3)
                    ml(TILES, NS, 0, 16 * (TILES // 2 + 1))
                phase()
                dve.memset(ssum[:, :], 0.0).then_inc(S("filled"), 1)
                dve.wait_ge(S("filled"), 2 * l + 2)
                with dve.Fori(0, KT // 2) as i:
                    for k in range(2):
                        lo(i * 2 + (U0[l] + U_IN + k + 1), (k + 1) % 2)
                        dve.wait_ge(S("squared"), i * 2 + (KT * (4 * l + 1) + k + 1))
                        dve.wait_ge(S("squares_added"), i * 2 + (KT * (4 * l + 1) + k))
                        dve.tensor_tensor(ssum[:, :], ssum[:, :], sq2[:, k], ALU.add).then_inc(S("squares_added"), 1)
                post_norm(4 * l + 1, added=True)
                pre_norm(4 * l + 2, 2 * l + 1)
                phase()
                dve.wait_ge(S("acc_zero"), l + 1)
                with dve.Fori(0, FG - 1) as g:
                    ff_group(l, g, False)
                ff_group(l, FG - 1, l == 1)
                phase()
                post_norm(4 * l + 3)
            phase()

        @block.gpsimd
        def _(pool):
            dma = pool.dma_start

            def affine(v, pattern, op, fill, base, mult):
                return pool.affine_select(out=v, in_=v, pattern=pattern, compare_op=op, fill=fill, base=base,
                                          channel_multiplier=mult)

            done = [0]

            def step(ins):
                done[0] += 1
                ins.then_inc(S("const_step"), 1)
                pool.wait_ge(S("const_step"), done[0])

            def constants():
                step(pool.memset(ident[:, :], 0.0))
                step(affine(ident[:, :], [[-1, P]], ALU.not_equal, 1.0, 0, 1))
                pool.sem_inc(S("ident_ready"), 1)
                pool.memset(ones[:, :], 1.0)
                pool.memset(triU[:, :], 1.0)
                pool.memset(maskpos[:, :], 0.0)
                pool.memset(masknegT[:, :], 0.0)
                pool.memset(triUS[:, :], 1.0)
                pool.memset(maskposS[:, :], 0.0)
                pool.memset(masknegTS[:, :], 0.0)
                pool.memset(blk4[:, :], 1.0)
                pool.memset(rowmask[:, :], 1.0)
                pool.memset(colmask[:, :, :], 0.0)
                pool.memset(sel[:, :, :], 0.0)
                step(pool.memset(lmask[:, :, :], 0.0))
                for m, n in ((triU, P), (triUS, NS)):
                    step(affine(m[:, :], [[1, n]], ALU.is_ge, 0.0, 0, -1))
                for m, n in ((maskpos, P), (maskposS, NS)):
                    step(affine(m[:, :], [[-1, n]], ALU.is_gt, BIG, 0, 1))
                for m, n in ((masknegT, P), (masknegTS, NS)):
                    step(affine(m[:, :], [[1, n]], ALU.is_ge, -BIG, 0, -1))
                for m, fill in ((triUS, 0.0), (maskposS, BIG), (masknegTS, -BIG), (blk4, 0.0)):
                    v = m[:, :].rearrange("p (b s) -> p b s", s=LS)
                    step(affine(v, [[-LS, NB], [0, LS]], ALU.is_ge, fill, 0, 1))
                    step(affine(v, [[LS, NB], [0, LS]], ALU.is_ge, fill, LS - 1, -1))
                step(affine(rowmask[:, :], [[-LS, NB]], ALU.is_ge, 0.0, 0, 1))
                step(affine(rowmask[:, :], [[LS, NB]], ALU.is_ge, 0.0, LS - 1, -1))
                for b in range(NB):
                    step(pool.memset(colmask[:, b, b * LS:(b + 1) * LS], 1.0))
                step(affine(sel[:, :, :], [[-1, H], [0, P]], ALU.not_equal, 1.0, 0, 1))
                for q in range(LEVELS):
                    w = 1 << q
                    v = lmask[:, q, :].rearrange("p (b e w) -> p b e w", e=2, w=w)
                    step(pool.memset(v[:, :, 1, :], 1.0))
                    pat = lambda a: [[a, P // (2 * w)], [0, w]]
                    step(affine(v[:, :, 1, :], pat(-2 * w), ALU.is_ge, 0.0, 0, 1))
                    step(affine(v[:, :, 1, :], pat(2 * w), ALU.is_ge, 0.0, w - 1, -1))

            def load_x():
                r = rows_in
                step(pool.memset(r[:, :], 0.0))
                dma(r[0:64, :], norm_g.rearrange("l q (c p) -> (l q c) p", p=P)).then_inc(S("rows_loaded"), 16)
                dma(r[64:112, :], conv_w.rearrange("e j (c p) -> (e j c) p", p=P)).then_inc(S("rows_loaded"), 16)
                dma(r[112:113, :], gdn_norm_g).then_inc(S("rows_loaded"), 16)
                dma(r[113:117, :], sgu_norm_g[0]).then_inc(S("rows_loaded"), 16)
                dma(r[117:119, :], mlstm_norm_g.rearrange("e (c p) -> (e c) p", p=P)).then_inc(S("rows_loaded"), 16)
                dma(r[119:123, :], sgu_b[0]).then_inc(S("rows_loaded"), 16)

            def residual(p):
                for c in range(KT):
                    pool.wait_ge(S("mix_normed"), KT * p + c + 1)
                    pool.tensor_tensor(xT[:, c, RS:T], xT[:, c, RS:T], hf2[:, c % 2, RS:T], ALU.add)\
                        .then_inc(S("x_ready"), 1)

            def in_proj(l):
                pr = proj[l]
                if l == 0:
                    dma(cs_tm[0:24, :], state_gdn_conv[0].rearrange("b j c -> (b j) c")).then_inc(S("wg_loaded"), 16)
                dma(wg[:, :, :], w_in[l][0, :, GATE0:GATE0 + 2 * H].rearrange("(t p) n -> p t n", p=P))\
                    .then_inc(S("wg_loaded"), 16)

                def send(i, c0, k):
                    dst = pr[bass.ds(i * 2 + (c0 + k), 1)].rearrange("a p t -> (a p) t")
                    dma(dst, pout2[:, k]).then_inc(S("stored"), 16)
                    pool.wait_ge(S("stored"), i * 32 + 16 * (l * NCH + c0 + k + 1))
                    pool.sem_inc(S("row_free"), 1)

                if l == 0:
                    with pool.Fori(0, NCONV // 2) as i:
                        for k in range(2):
                            pool.wait_ge(S("conv_act"), i * 2 + (2 + k + 1))
                            send(i, 0, k)
                    first = NCONV
                else:
                    first = 0
                with pool.Fori(0, (NCH - first) // 2) as i:
                    for k in range(2):
                        pool.wait_ge(S("act_evac"), i * 6 + (AE0[l] + BANKS + (first + k + 1) * TG))
                        send(i, first, k)
                if l == 0:
                    pool.wait_ge(S("tails_sb"), 1)
                    dma(conv_p[0, 0], tail_tm[0:3, :]).then_inc(S("state_out"), 16)
                    dma(conv_s[0].rearrange("b j c -> (b j) c"), tail_tm[3:27, :]).then_inc(S("state_out"), 16)
                    pool.wait_ge(S("state_out"), 32)

            def gdn_prep():
                pool.wait_ge(S("sgw_loaded"), 16 * (4 + NB))
                step(pool.tensor_copy(BROWS[0:1, :, 1:, :], BROWS[0:1, :, 0:1, :].broadcast_to([1, H, NB - 1, LS])))

            def tile_in(l, t, n, X, name, c0=0, c1=NCH):
                src = proj[l][c0:c1, :, bass.ds(t * P, n)].rearrange("c p t -> p c t")
                dma(X[:, c0:c1], src).then_inc(S(name), 16)

            def gdn_early(t, n, X):
                tile_in(0, t, n, X, "g_xin", 0, 12)
                tile_in(0, t, n, X, "g_xin", 20, NCH)

            def gating_v(t, n):
                VB = gdn_map(n)["VB"]
                pool.wait_ge(S("g_vsr"), t + 1)
                pool.tensor_tensor(VB[0:n], VB[0:n], GSG[0:n], ALU.mult).then_inc(S("g_vb"), 1)

            def out_state(m, h):
                cs = m["CS2"][:, h % 2]
                pool.wait_ge(S("ms_upd"), (h + 1) * NB)
                dma(c_s[0, :, h].rearrange("b k v -> k b v"), cs[:, :, 0:DV]).then_inc(S(f"cs_out{h % 2}"), 16)
                with nc.allow_non_contiguous_dma("1024 numbers"):
                    dma(n_s[0, :, h].rearrange("b k -> k b").unsqueeze(2), cs[:, :, DV:DV + 1])\
                        .then_inc(S(f"cs_out{h % 2}"), 16)

            load_x()
            constants()
            dma(hvec[:, 0, :], a_log.broadcast_to([P, H])).then_inc(S("hvec_loaded"), 16)
            dma(hvec[:, 1, :], dt_bias.broadcast_to([P, H])).then_inc(S("hvec_loaded"), 16)
            pool.sem_inc(S("w_used"), 2)
            pool.sem_inc(S("row_free"), 2)
            phase = lambda: phase_end(pool, "pool")
            for l in range(2):
                phase()
                in_proj(l)
                phase()
                if l == 0:
                    X = gdn_map(P)["X"]
                    gdn_early(0, P, X)
                    tile_in(0, 0, P, X, "g_xgate", 12, 20)
                    gdn_prep()
                    phase()
                    with pool.Fori(0, TILES - 1) as t:
                        gating_v(t, P)
                        pool.wait_ge(S("g_qk"), t + 1)
                        gdn_early(t + 1, P, X)
                        pool.wait_ge(S("g_ofa"), t + 1)
                        pool.wait_ge(S("g_ofb"), t + 1)
                        tile_in(0, t + 1, P, X, "g_xgate", 12, 20)
                    gating_v(TILES - 1, P)
                    pool.wait_ge(S("g_state"), TILES + 1)
                    dma(gdn_p[0, 0].rearrange("h k v -> k h v"), St[:, :, :]).then_inc(S("state_out"), 16)
                    phase()
                    m = gdn_map(NS)
                    gdn_early(TILES, NS, m["X"])
                    tile_in(0, TILES, NS, m["X"], "g_xgate", 12, 20)
                    dma(m["SS"], state_gdn[0].rearrange("b h k v -> k b h v")).then_inc(S("wg_loaded"), 16)
                    gating_v(TILES, NS)
                    pool.wait_ge(S("g_vb"), TILES + 1)
                    dma(sguv_s[0].rearrange("b s c -> (b s) c"), m["VB"][0:NS].rearrange("p g c -> p (g c)"))\
                        .then_inc(S("state_out"), 16)
                    pool.wait_ge(S("gs_new"), H)
                    dma(gdn_s[0].rearrange("b h k v -> k b h v"), m["SS"]).then_inc(S("state_out"), 16)
                    pool.wait_ge(S("state_out"), 16 * 5)
                else:
                    dma(hvec[:, 0:2, :], gate_b_odd.rearrange("e (a h) -> e a h", a=2).broadcast_to([P, 2, H]))\
                        .then_inc(S("hvec_loaded"), 16)
                    with nc.allow_non_contiguous_dma("32 numbers"):
                        dma(MPR[0:H, NB:2 * NB].unsqueeze(2), state_mlstm_m[0].rearrange("b h -> h b").unsqueeze(2))\
                            .then_inc(S("hvec_loaded"), 16)
                    pool.wait_ge(S("m_row_step"), 10)
                    with nc.allow_non_contiguous_dma("36 numbers"):
                        dma(m_p[0, 0:1].rearrange("b h -> h b"), MLA[0:H, TILES - 1:TILES]).then_inc(S("state_out"), 16)
                        dma(m_s[0].rearrange("b h -> h b").unsqueeze(2), MLA[0:H, TILES:2 * NB].unsqueeze(2))\
                            .then_inc(S("state_out"), 16)
                    pool.wait_ge(S("state_out"), 16 * 7)
                    phase()
                    step(pool.memset(ml_map(P)["V1"][:, :, DV:DV + 1], 1.0))
                    for k in range(2):
                        tile_in(1, k, P, ml_map(P, k)["X"], f"m_xin{k}")
                    with pool.Fori(0, TILES // 2 - 1) as i:
                        for k in range(2):
                            pool.wait_ge(S("g_ofb"), i * 2 + (k + TILES + 2))
                            tile_in(1, i * 2 + (k + 2), P, ml_map(P, k)["X"], f"m_xin{k}")
                    pool.wait_ge(S("g_state"), 2 * TILES + 2)
                    dma(c_p[0, 0].rearrange("h k v -> k h v"), CN[:, :, 0:DV]).then_inc(S("state_out"), 16)
                    with nc.allow_non_contiguous_dma("512 numbers"):
                        dma(n_p[0, 0].rearrange("h k -> k h").unsqueeze(2), CN[:, :, DV:DV + 1])\
                            .then_inc(S("state_out"), 16)
                    phase()
                    m = ml_map(NS)
                    tile_in(1, TILES, NS, m["X"], "m_xin0")
                    for h in range(H):
                        cs = m["CS2"][:, h % 2]
                        if h >= 2:
                            pool.wait_ge(S(f"cs_out{h % 2}"), 32 * (h // 2))
                        dma(cs[:, :, 0:DV], state_mlstm_c[0, :, h].rearrange("b k v -> k b v"))\
                            .then_inc(S(f"ms_cin{h % 2}"), 16)
                        with nc.allow_non_contiguous_dma("1024 numbers"):
                            dma(cs[:, :, DV:DV + 1], state_mlstm_n[0, :, h].rearrange("b k -> k b").unsqueeze(2))\
                                .then_inc(S(f"ms_cin{h % 2}"), 16)
                        if h >= 1:
                            out_state(m, h - 1)
                    out_state(m, H - 1)
                    pool.wait_ge(S("state_out"), 16 * 9)
                    for k in range(2):
                        pool.wait_ge(S(f"cs_out{k}"), 64)
                phase()
                residual(2 * l)
                pool.memset(acc[:, :, :], 0.0).then_inc(S("acc_zero"), 1)
                phase()
                phase()
                residual(2 * l + 1)
            phase()
            for t in range(TILES + 1):
                pool.wait_ge(S("y_copied"), 2 * t + 2)
                n = P if t < TILES else NS
                dst = y_prompt[0, t * P:(t + 1) * P, :] if t < TILES else y_sample.rearrange("b s d -> (b s) d")
                dma(dst, x_tm[0:n, t % 2, :]).then_inc(S(f"y_stored{t % 2}"), 16)
            pool.wait_ge(S("y_stored0"), 16 * 5)
            pool.wait_ge(S("y_stored1"), 16 * 4)


_INS = ['x_prompt', 'x_sample', 'state_gdn', 'state_gdn_conv', 'state_mlstm_c', 'state_mlstm_n', 'state_mlstm_m',
        'norm_g', 'w_in_even', 'conv_w', 'a_log', 'dt_bias', 'gdn_norm_g', 'sgu_norm_g', 'sgu_w', 'sgu_b',
        'w_out_even', 'w_in_odd', 'gate_b_odd', 'mlstm_norm_g', 'w_out_odd', 'w_ff1', 'w_ff2']
_OUTS = [(1, 1024, 1024), (8, 4, 1024), (1, 1, 4, 128, 128), (1, 8, 4, 128, 128), (1, 1, 3, 1536), (1, 8, 3, 1536),
         (1, 8, 4, 512), (1, 1, 4, 128, 256), (1, 8, 4, 128, 256), (1, 1, 4, 128), (1, 8, 4, 128), (1, 1, 4),
         (1, 8, 4)]


def kernel(**inputs):
    import numpy as _np
    import concourse.bacc as _bacc
    from concourse import mybir as _mybir
    from concourse.bass_utils import run_bass_kernel_spmd as _run

    nc = _bacc.Bacc("TRN2", target_bir_lowering=False, num_devices=1)
    arrays, args = {}, []
    for name in _INS:
        a = _np.ascontiguousarray(inputs[name])
        arrays[f"in_{name}_dram"] = a
        args.append(nc.dram_tensor(f"in_{name}_dram", a.shape, _mybir.dt.from_np(a.dtype), kind="ExternalInput").ap())
    for i, shape in enumerate(_OUTS):
        args.append(nc.dram_tensor(f"out_{i}_dram", shape, _mybir.dt.float32, kind="ExternalOutput").ap())
    build(nc, *args)
    r = _run(nc, [arrays], core_ids=[0])
    return tuple(r.results[0][f"out_{i}_dram"] for i in range(len(_OUTS)))
```
